# Optimizing a Trainium2 kernel written in Bass

```python
import jax, jax.numpy as jnp
from jax import lax
import numpy as np

D_MODEL = 1024
BATCH = 1
SEQ = 1024
DEPTH = 1

N_MIXERS = 3
NORM_EPS = 1e-6
L2_EPS = 1e-6
BRANCH = 2 * D_MODEL

GDN_DK = 128
GDN_HEADS = D_MODEL // GDN_DK
GDN_DV = BRANCH // GDN_HEADS
GDN_QK = GDN_HEADS * GDN_DK
GDN_V = GDN_HEADS * GDN_DV
GDN_CONV = 4
GDN_CHUNK = 64
GDN_SPLITS = (GDN_QK, GDN_QK, GDN_V, GDN_V, GDN_HEADS, GDN_HEADS)
GDN_IN = sum(GDN_SPLITS)

HGRN_DK = 128
HGRN_HEADS = D_MODEL // HGRN_DK
HGRN_DV = BRANCH // HGRN_HEADS
HGRN_F = HGRN_HEADS * HGRN_DK
HGRN_V = HGRN_HEADS * HGRN_DV
HGRN_CHUNK = 16
HGRN_SPLITS = (HGRN_F, HGRN_F, HGRN_V, HGRN_V)
HGRN_IN = sum(HGRN_SPLITS)

RWKV_DH = 64
RWKV_HEADS = BRANCH // RWKV_DH
RWKV_DECAY_LORA = 64
RWKV_AAA_LORA = 64
RWKV_SPLITS = (BRANCH, BRANCH, BRANCH, BRANCH, RWKV_DECAY_LORA, RWKV_AAA_LORA)
RWKV_IN = sum(RWKV_SPLITS)
RWKV_GN_EPS = RWKV_DH * 1e-5

N_GDN = (DEPTH + N_MIXERS - 1) // N_MIXERS
N_HGRN = (DEPTH + N_MIXERS - 2) // N_MIXERS
N_RWKV = DEPTH // N_MIXERS

kernel_name = "hybrid_gdn_hgrn2_rwkv7_interleaved"

def split_cols(p, sizes):
    idx = [int(s) for s in np.cumsum(sizes)[:-1]]
    return jnp.split(p, idx, axis=-1)

def rms_norm(x, w, eps=NORM_EPS):
    xf = x.astype(jnp.float32)
    return xf * lax.rsqrt(jnp.mean(xf * xf, axis=-1, keepdims=True) + eps) * w

def l2_norm(x, eps=L2_EPS):
    return x * lax.rsqrt(jnp.sum(x * x, axis=-1, keepdims=True) + eps)

def causal_short_conv(x, w):
    K = w.shape[0]
    T = x.shape[1]
    xp = jnp.pad(x, ((0, 0), (K - 1, 0), (0, 0)))
    out = xp[:, 0:T] * w[0]
    for j in range(1, K):
        out = out + xp[:, j:j + T] * w[j]
    return out

def to_chunks(t, size):
    b, T, h = t.shape[:3]
    t = t.reshape((b, T // size, size, h) + t.shape[3:])
    return jnp.moveaxis(t, 3, 1)

def from_chunks(t):
    b, h, n, c, d = t.shape
    return t.transpose(0, 2, 3, 1, 4).reshape(b, n * c, h, d)

def gated_delta_rule_chunked(q, k, v, beta, g):
    bsz, T, H, dk = q.shape
    dv = v.shape[-1]
    C = GDN_CHUNK
    q, k, v = to_chunks(q, C), to_chunks(k, C), to_chunks(v, C)
    beta, g = to_chunks(beta, C), to_chunks(g, C)
    gc = jnp.cumsum(g, axis=-1)
    incl = jnp.tril(jnp.ones((C, C), bool))
    strict = jnp.tril(jnp.ones((C, C), bool), -1)
    rel = gc[..., :, None] - gc[..., None, :]
    decay = jnp.exp(jnp.where(incl, rel, -jnp.inf))
    kb = k * beta[..., None]
    A = jnp.where(strict, jnp.einsum('bhnid,bhnjd->bhnij', kb, k) * decay, 0.0)
    tri = A + jnp.eye(C, dtype=A.dtype)
    rhs = jnp.concatenate([v * beta[..., None], kb * jnp.exp(gc)[..., None]], axis=-1)
    sol = lax.linalg.triangular_solve(tri, rhs, left_side=True, lower=True, unit_diagonal=True)
    u, w = sol[..., :dv], sol[..., dv:]
    attn = jnp.einsum('bhnid,bhnjd->bhnij', q, k) * decay
    q_dec = q * jnp.exp(gc)[..., None]
    k_dec = k * jnp.exp(gc[..., -1:] - gc)[..., None]
    g_last = jnp.exp(gc[..., -1])

    def step(S, inp):
        q_c, a_c, u_c, w_c, k_c, gl_c = inp
        v_new = u_c - jnp.einsum('bhck,bhkv->bhcv', w_c, S)
        o_c = jnp.einsum('bhck,bhkv->bhcv', q_c, S) + jnp.einsum('bhij,bhjv->bhiv', a_c, v_new)
        S = S * gl_c[..., None, None] + jnp.einsum('bhck,bhcv->bhkv', k_c, v_new)
        return S, o_c

    xs = tuple(jnp.moveaxis(t, 2, 0) for t in (q_dec, attn, u, w, k_dec, g_last))
    S0 = jnp.zeros((bsz, H, dk, dv), jnp.float32)
    _, o = lax.scan(step, S0, xs)
    return from_chunks(jnp.moveaxis(o, 0, 2))

def gdn_mixer(h, w_in, conv_w, a_log, dt_bias, norm_w, w_out):
    bsz, T, _ = h.shape
    p = (h @ w_in).astype(jnp.float32)
    qkv, z, b, a = split_cols(p, (2 * GDN_QK + GDN_V, GDN_V, GDN_HEADS, GDN_HEADS))
    qkv = jax.nn.silu(causal_short_conv(qkv, conv_w))
    q, k, v = split_cols(qkv, (GDN_QK, GDN_QK, GDN_V))
    q = l2_norm(q.reshape(bsz, T, GDN_HEADS, GDN_DK)) * (GDN_DK ** -0.5)
    k = l2_norm(k.reshape(bsz, T, GDN_HEADS, GDN_DK))
    v = v.reshape(bsz, T, GDN_HEADS, GDN_DV)
    beta = jax.nn.sigmoid(b)
    g = -jnp.exp(a_log) * jax.nn.softplus(a + dt_bias)
    o = gated_delta_rule_chunked(q, k, v, beta, g)
    o = rms_norm(o, norm_w) * jax.nn.silu(z.reshape(bsz, T, GDN_HEADS, GDN_DV))
    return o.reshape(bsz, T, GDN_V) @ w_out

def gla_chunked(q, k, v, log_f):
    bsz, T, H, dk = q.shape
    dv = v.shape[-1]
    C = HGRN_CHUNK
    q, k, v, lf = (to_chunks(t, C) for t in (q, k, v, log_f))
    G = jnp.cumsum(lf, axis=3)
    ref = G[..., C // 2:C // 2 + 1, :]
    incl = jnp.tril(jnp.ones((C, C), bool))
    attn = jnp.einsum('bhnid,bhnjd->bhnij', q * jnp.exp(G - ref), k * jnp.exp(ref - G))
    attn = jnp.where(incl, attn, 0.0)
    o_intra = jnp.einsum('bhnij,bhnjv->bhniv', attn, v)
    q_dec = q * jnp.exp(G)
    k_dec = k * jnp.exp(G[..., -1:, :] - G)
    g_last = jnp.exp(G[..., -1, :])

    def step(S, inp):
        q_c, k_c, v_c, gl_c = inp
        o_c = jnp.einsum('bhck,bhkv->bhcv', q_c, S)
        S = S * gl_c[..., None] + jnp.einsum('bhck,bhcv->bhkv', k_c, v_c)
        return S, o_c

    xs = tuple(jnp.moveaxis(t, 2, 0) for t in (q_dec, k_dec, v, g_last))
    S0 = jnp.zeros((bsz, H, dk, dv), jnp.float32)
    _, o_inter = lax.scan(step, S0, xs)
    return from_chunks(o_intra + jnp.moveaxis(o_inter, 0, 2))

def hgrn2_mixer(h, w_in, lower_bound, norm_w, w_out):
    bsz, T, _ = h.shape
    p = (h @ w_in).astype(jnp.float32)
    q, f, i, z = split_cols(p, HGRN_SPLITS)
    lb = lower_bound
    log_f = jnp.logaddexp(jnp.log(lb), jnp.log1p(-lb) + jax.nn.log_sigmoid(f))
    k = (1.0 - lb) * jax.nn.sigmoid(-f)
    q = jax.nn.silu(q)
    shp_k = (bsz, T, HGRN_HEADS, HGRN_DK)
    o = gla_chunked(q.reshape(shp_k), k.reshape(shp_k),
                    i.reshape(bsz, T, HGRN_HEADS, HGRN_DV), log_f.reshape(shp_k))
    o = rms_norm(o, norm_w) * jax.nn.silu(z.reshape(bsz, T, HGRN_HEADS, HGRN_DV))
    return o.reshape(bsz, T, HGRN_V) @ w_out

def rwkv7_scan(r, w, k, v, kk, a):
    bsz, T, H, N = r.shape

    def step(S, inp):
        r_t, w_t, k_t, v_t, kk_t, a_t = inp
        sa = jnp.einsum('bhvk,bhk->bhv', S, -kk_t)
        S = (S * w_t[:, :, None, :] + sa[..., None] * (kk_t * a_t)[:, :, None, :]
             + v_t[..., None] * k_t[:, :, None, :])
        return S, jnp.einsum('bhvk,bhk->bhv', S, r_t)

    xs = tuple(jnp.moveaxis(t, 1, 0) for t in (r, w, k, v, kk, a))
    S0 = jnp.zeros((bsz, H, N, N), jnp.float32)
    _, y = lax.scan(step, S0, xs)
    return jnp.moveaxis(y, 0, 1)

def rwkv7_mixer(h, w_in, mu, w0, w_lora_up, a0, a_lora_up, k_k, k_a, r_k, ln_w, ln_b, w_out):
    bsz, T, _ = h.shape
    p = (h @ w_in).astype(jnp.float32)
    p_prev = jnp.pad(p, ((0, 0), (1, 0), (0, 0)))[:, :-1]
    p = p + (p_prev - p) * mu
    r, k, v, z, wd, ad = split_cols(p, RWKV_SPLITS)
    w_log = -jax.nn.softplus(-(w0 + jnp.tanh(wd) @ w_lora_up)) - 0.5
    decay = jnp.exp(-jnp.exp(w_log))
    a = jax.nn.sigmoid(a0 + ad @ a_lora_up)
    shp = (bsz, T, RWKV_HEADS, RWKV_DH)
    kk = l2_norm((k * k_k).reshape(shp), eps=1e-12)
    k = k * (1.0 + (a - 1.0) * k_a)
    r, k, v, decay, a = (t.reshape(shp) for t in (r, k, v, decay, a))
    y = rwkv7_scan(r, decay, k, v, kk, a)
    mean = jnp.mean(y, axis=-1, keepdims=True)
    var = jnp.mean(jnp.square(y - mean), axis=-1, keepdims=True)
    y = ((y - mean) * lax.rsqrt(var + RWKV_GN_EPS)).reshape(bsz, T, BRANCH) * ln_w + ln_b
    bonus = jnp.sum(r * k * r_k, axis=-1, keepdims=True) * v
    y = (y + bonus.reshape(bsz, T, BRANCH)) * jax.nn.silu(z)
    return y @ w_out

def setup_inputs(seed: int = 0) -> dict:
    key = jax.random.key(seed)
    ks = iter(jax.random.split(key, 32))
    nrm = lambda shape, s: jax.random.normal(next(ks), shape, jnp.float32) * s
    uni = lambda shape, lo, hi: jax.random.uniform(next(ks), shape, jnp.float32, lo, hi)
    D = D_MODEL
    dt = jnp.exp(uni((N_GDN, GDN_HEADS), float(np.log(1e-3)), float(np.log(1e-1))))
    return {
        "x": nrm((BATCH, SEQ, D), 1.0),
        "c": nrm((BATCH, D), 1.0),
        "ada_w": nrm((DEPTH, D, 3 * D), 0.5 * D ** -0.5),
        "ada_b": nrm((DEPTH, 3 * D), 0.1),
        "norm_w": 1.0 + nrm((DEPTH, D), 0.02),
        "gdn_w_in": nrm((N_GDN, D, GDN_IN), D ** -0.5),
        "gdn_conv_w": nrm((N_GDN, GDN_CONV, 2 * GDN_QK + GDN_V), GDN_CONV ** -0.5),
        "gdn_a_log": jnp.log(uni((N_GDN, GDN_HEADS), 1.0, 16.0)),
        "gdn_dt_bias": dt + jnp.log(-jnp.expm1(-dt)),
        "gdn_norm_w": 1.0 + nrm((N_GDN, GDN_DV), 0.02),
        "gdn_w_out": nrm((N_GDN, GDN_V, D), GDN_V ** -0.5),
        "hgrn_w_in": nrm((N_HGRN, D, HGRN_IN), D ** -0.5),
        "hgrn_lb_logits": nrm((DEPTH, HGRN_F), 0.1),
        "hgrn_norm_w": 1.0 + nrm((N_HGRN, HGRN_DV), 0.02),
        "hgrn_w_out": nrm((N_HGRN, HGRN_V, D), HGRN_V ** -0.5),
        "rwkv_w_in": nrm((N_RWKV, D, RWKV_IN), D ** -0.5),
        "rwkv_mu": uni((N_RWKV, RWKV_IN), 0.0, 1.0),
        "rwkv_w0": uni((N_RWKV, BRANCH), -6.0, -1.0),
        "rwkv_w_lora_up": nrm((N_RWKV, RWKV_DECAY_LORA, BRANCH), 0.5 * RWKV_DECAY_LORA ** -0.5),
        "rwkv_a0": nrm((N_RWKV, BRANCH), 0.1),
        "rwkv_a_lora_up": nrm((N_RWKV, RWKV_AAA_LORA, BRANCH), 0.5 * RWKV_AAA_LORA ** -0.5),
        "rwkv_k_k": 0.85 + nrm((N_RWKV, BRANCH), 0.02),
        "rwkv_k_a": 1.0 + nrm((N_RWKV, BRANCH), 0.02),
        "rwkv_r_k": nrm((N_RWKV, RWKV_HEADS, RWKV_DH), 0.1),
        "rwkv_ln_w": 1.0 + nrm((N_RWKV, BRANCH), 0.02),
        "rwkv_ln_b": nrm((N_RWKV, BRANCH), 0.02),
        "rwkv_w_out": nrm((N_RWKV, BRANCH, D), BRANCH ** -0.5),
        "final_norm_w": 1.0 + nrm((D,), 0.02),
    }

def reference(x, c, ada_w, ada_b, norm_w,
              gdn_w_in, gdn_conv_w, gdn_a_log, gdn_dt_bias, gdn_norm_w, gdn_w_out,
              hgrn_w_in, hgrn_lb_logits, hgrn_norm_w, hgrn_w_out,
              rwkv_w_in, rwkv_mu, rwkv_w0, rwkv_w_lora_up, rwkv_a0, rwkv_a_lora_up,
              rwkv_k_k, rwkv_k_a, rwkv_r_k, rwkv_ln_w, rwkv_ln_b, rwkv_w_out,
              final_norm_w):
    c_act = jax.nn.silu(c.astype(jnp.float32))
    lb_p = jax.nn.softmax(hgrn_lb_logits.astype(jnp.float32), axis=0)
    lower_bounds = jnp.cumsum(lb_p, axis=0) - lb_p[0]
    for i in range(DEPTH):
        mod = c_act @ ada_w[i] + ada_b[i]
        shift, scale, gate = jnp.split(mod, 3, axis=-1)
        h = rms_norm(x, norm_w[i]) * (1.0 + scale[:, None, :]) + shift[:, None, :]
        j = i // N_MIXERS
        kind = i % N_MIXERS
        if kind == 0:
            y = gdn_mixer(h, gdn_w_in[j], gdn_conv_w[j], gdn_a_log[j], gdn_dt_bias[j],
                          gdn_norm_w[j], gdn_w_out[j])
        elif kind == 1:
            y = hgrn2_mixer(h, hgrn_w_in[j], lower_bounds[i], hgrn_norm_w[j], hgrn_w_out[j])
        else:
            y = rwkv7_mixer(h, rwkv_w_in[j], rwkv_mu[j], rwkv_w0[j], rwkv_w_lora_up[j],
                            rwkv_a0[j], rwkv_a_lora_up[j], rwkv_k_k[j], rwkv_k_a[j],
                            rwkv_r_k[j], rwkv_ln_w[j], rwkv_ln_b[j], rwkv_w_out[j])
        x = (x + gate[:, None, :] * y).astype(x.dtype)
    return rms_norm(x, final_norm_w).astype(x.dtype)


_drawn_inputs = setup_inputs


def setup_inputs(seed=0):
    import zlib

    import numpy as np

    out = dict(_drawn_inputs(seed))
    spreads = {}
    factors = {'norm_w': 8.0, 'gdn_norm_w': 8.0, 'final_norm_w': 3.112}
    for name, (base, spread) in spreads.items():
        noise = np.random.default_rng([zlib.crc32(name.encode()), seed]).standard_normal(out[name].shape)
        drawn = base * np.exp(spread * noise) if base else spread * noise
        out[name] = __import__('jax').numpy.asarray(drawn.astype(out[name].dtype))
    for name, factor in factors.items():
        out[name] = (out[name] * factor).astype(out[name].dtype)
    return out
```

```python
from contextlib import ExitStack

import concourse.bass as bass
from concourse import mybir

F32 = mybir.dt.float32
F32R = mybir.dt.float32r
ALU = mybir.AluOpType
ACT = mybir.ActivationFunctionType

P = 128
D_MODEL = 1024
SEQ = 1024
HEADS = 8
DK = 128
DV = 256
NORM_EPS = 1e-6
L2_EPS = 1e-6

KT = D_MODEL // P
UNITS = 2 * HEADS
HALF = SEQ // 2
NCH = HALF // P
TILES = SEQ // P
TAPS = 4
PIECES = 6
CONVED = 4
WTILES = 8
MM = 3 * KT
Z_OFF = 2 * HEADS * DK + HEADS * DV
BA_OFF = Z_OFF + HEADS * DV
BLK = 16
NBLK = P // BLK


def build(nc, x, c, ada_w, ada_b, norm_w, w_in, conv_w, a_log, dt_bias, gdn_norm_w, w_out,
          final_norm_w, out):
    ctx = ExitStack()
    with ctx:
        def sb(name, shape, dt=F32):
            return ctx.enter_context(nc.sbuf_tensor(name, shape, dt))

        def sem(name):
            return ctx.enter_context(nc.semaphore(name))

        h_hi = sb("h_hi", [P, KT, SEQ], F32R)
        h_lo = sb("h_lo", [P, KT, SEQ], F32R)
        y = sb("y", [P, TILES, D_MODEL])
        w_raw = sb("w_raw", [P, 2, 1024])
        w_hi = sb("w_hi", [P, 2, KT, P], F32R)
        w_lo = sb("w_lo", [P, 2, KT, P], F32R)
        wo_hi = sb("wo_hi", [P, 2, D_MODEL], F32R)
        wo_lo = sb("wo_lo", [P, 2, D_MODEL], F32R)
        og_hi = sb("og_hi", [P, 2, P], F32R)
        og_lo = sb("og_lo", [P, 2, P], F32R)
        gate_bc = sb("gate_bc", [P, D_MODEL])
        pre = sb("pre", [P, 2, HALF + 4])
        work = sb("work", [P, 12288])
        t16 = sb("t16", [P, NCH, P])
        u16 = sb("u16", [P, NCH, P])
        ident = sb("ident", [P, P])
        upto = sb("upto", [P, P])
        after = sb("after", [P, P])
        lower = sb("lower", [P, P])
        pair_mask = sb("pair_mask", [P, 3, P])
        ones = sb("ones", [P, P])
        fss = sb("fss", [P, TILES])
        frs = sb("frs", [P, TILES])
        cw = sb("cw", [P, TAPS * 32])
        rows_t = sb("rows_t", [P, 34])
        mod = sb("mod", [P, 24])
        g_tab = sb("g_tab", [P, UNITS, NCH])
        beta = sb("beta", [P, UNITS, NCH])
        e_gc = sb("e_gc", [P, UNITS, NCH])
        e_kd = sb("e_kd", [P, UNITS, NCH])
        e_gl = sb("e_gl", [P, UNITS, NCH])
        even = sb("even", [P, UNITS])
        odd = sb("odd", [P, UNITS])
        tails = sb("tails", [P, CONVED, 4])
        st = sb("st", [P, 2 * NCH])
        rs = sb("rs", [P, 2 * NCH])
        sc = sb("sc", [P, 6, NCH])
        oss = sb("oss", [P, 4])
        neg_half = sb("neg_half", [P, 8])
        l2_eps4 = sb("l2_eps4", [P, 2 * NCH])
        small = sb("small", [P, 64])
        blk_id = sb("blk_id", [NBLK * NCH, BLK, BLK])
        state = sb("state", [P, DV])

        def part(at, n, **dims):
            v = work[:, at:at + n]
            return v.rearrange(dims.pop("to"), **dims) if dims else v

        fin = part(0, 2048, to="p (s d) -> p s d", s=2)
        cv = part(0, 2048, to="p (m t) -> p m t", m=4)
        th = part(2048, 2048, to="p (m t) -> p m t", m=4)
        kq = part(4096, 1024, to="p (c t) -> p c t", c=NCH)
        vt = part(5120, 1024, to="p (c t) -> p c t", c=NCH)
        kdec = part(6144, 512, to="p (c t) -> p c t", c=NCH)
        attn_t = part(6656, 512, to="p (c t) -> p c t", c=NCH)
        u_fin = part(7168, 512, to="p (c t) -> p c t", c=NCH)
        zt = part(7680, 1024, to="p (m t) -> p m t", m=2)
        nmat = part(8704, 512, to="p (c t) -> p c t", c=NCH)
        decay = part(9216, 512, to="p (c t) -> p c t", c=NCH)
        g_after = part(9728, 512, to="p (c t) -> p c t", c=NCH)
        attn = part(10240, 512, to="p (c t) -> p c t", c=NCH)
        pmat = part(10752, 512, to="p (c t) -> p c t", c=NCH)
        tm = part(11264, 512, to="p (c t) -> p c t", c=NCH)
        um = part(11776, 512, to="p (c t) -> p c t", c=NCH)
        blk_n, blk_y, blk_yt, blk_tmp = (
            work[0:NBLK * NCH, o:o + BLK * BLK].rearrange("p (i j) -> p i j", i=BLK)
            for o in (9728, 9984, 9216, 9472))
        r_rhs = part(10240, 256)
        xs = part(10496, 256)
        qss = part(10752, 256)
        o_raw = part(11008, 256)
        o_n = part(11264, 256)
        og = part(11520, 256, to="p (m t) -> p m t", m=2)
        junk = part(11776, 256)
        junk_b = sb("junk_b", [P, P])
        ada_buf = part(0, 4096, to="p (s n) -> p s n", s=2)
        ada_acc = part(4096, 3072)
        gate_buf = part(4096, 2048, to="p (s n) -> p s n", s=2)
        xn = part(7168, 4096, to="p (c d) -> p c d", c=4)
        hf = part(11264, 1024, to="p (s t) -> p s t", s=2)
        rows = w_raw[:, 1, 0:2 * P].rearrange("p (r t) -> p r t", r=2)
        c_col = sb("c_col", [P, KT])
        c_th = sb("c_th", [P, KT])
        xss = sb("xss", [P, TILES])
        xrs = sb("xrs", [P, TILES])
        wba_raw = junk_b[:, :].rearrange("p (k n) -> p k n", k=KT)
        wba_hi = wo_hi[:, 0, 0:KT * 16].rearrange("p (k n) -> p k n", k=KT)
        wba_lo = wo_lo[:, 0, 0:KT * 16].rearrange("p (k n) -> p k n", k=KT)

        bank = [ctx.enter_context(nc.psum_tensor(f"bank{i}", [P, 512], F32)) for i in range(8)]

        PER = dict(
            w_gated=2, w_hi_done=8, w_lo_done=8,
            projected=6, evacuated=6, conv_done=4, tanh_done=6, silu_done=6,
            conv_step=16,
            turned=4, squared=8, turned_out=4,
            g_after_done=1, decay_mm=1, decay_exp=1, decay_done=1,
            norms_step=1, norms_done=1, scalar_step=4, scalars_done=1, v_scaled=4,
            gram_done=2, n_done=2, attn_done=2, attn_turned=1, attn_out=1,
            base_step=31, base_done=1,
            merge_p=3, merge_p_out=3, merge_d=3, merge_d_out=3,
            ks_done=4, qs_done=4, r_done=4, qs_scaled=4, x_done=4, x_out=4,
            kv_done=4, av_done=4, state_done=5, o_done=4, o_squared=4, o_mean=4, o_pow=4,
            o_scaled=4, o_turned=4, og_done=4, og_hi_done=4, og_lo_done=4,
            out_done=4, y_added=4,
        )
        S = {name: sem(name) for name in PER}
        MAKERS = dict(
            tensor="projected turned decay_mm gram_done attn_turned merge_p merge_d ks_done qs_done x_done "
                   "kv_done av_done o_turned out_done",
            scalar="w_hi_done evacuated tanh_done squared decay_exp attn_out qs_scaled x_out o_squared "
                   "og_hi_done",
            vector="w_gated conv_done silu_done conv_step turned_out scalar_step scalars_done n_done "
                   "attn_done base_step base_done merge_p_out merge_d_out r_done state_done o_done o_mean "
                   "o_scaled og_done y_added",
            gpsimd="w_lo_done g_after_done decay_done norms_step norms_done v_scaled o_pow og_lo_done",
        )
        raw_in = [sem(f"raw_in{i}") for i in range(2)]
        blk_in = sem("blk_in")
        n_stored = sem("n_stored")
        tu_stored = sem("tu_stored")
        blk_back = sem("blk_back")
        x_in = [sem(f"x_in{i}") for i in range(2)]
        ada_in = [sem(f"ada_in{i}") for i in range(2)]
        rows_in = sem("rows_in")
        c_in = sem("c_in")
        wba_in = sem("wba_in")
        bias_in = sem("bias_in")
        fw_in = sem("fw_in")
        stored = [sem(f"stored{i}") for i in range(2)]
        const_step = sem("const_step")
        consts = sem("consts")
        rows_turned, rows_out = sem("rows_turned"), sem("rows_out")
        c_step, x_squared, x_mean, x_pow = sem("c_step"), sem("x_squared"), sem("x_mean"), sem("x_pow")
        xn_done, x_turned, h_done, h_split = sem("xn_done"), sem("x_turned"), sem("h_done"), sem("h_split")
        hi_step = sem("hi_step")
        ada_summed, mod_mm, mod_done = sem("ada_summed"), sem("mod_mm"), sem("mod_done")
        wba_split, ba_mm, g_step, g_exp = sem("wba_split"), sem("ba_mm"), sem("g_step"), sem("g_exp")
        beta_step = sem("beta_step")
        sums_mm, tables_done, gate_mm, gate_done = (sem("sums_mm"), sem("tables_done"), sem("gate_mm"),
                                                     sem("gate_done"))
        fin_squared, fin_pow, fin_done, fin_step = (sem("fin_squared"), sem("fin_pow"), sem("fin_done"),
                                                    sem("fin_step"))

        def at(name, u, n):
            return PER[name] * (u + 1) + n

        def prime(eng, which):
            for name in MAKERS[which].split():
                eng.sem_inc(S[name], PER[name])

        def passed(eng, name, u, n):
            eng.wait_ge(S[name], at(name, u, n))

        def tile_landed(eng, u, k):
            eng.wait_ge(raw_in[k % 2], 16 * (4 * u + k // 2 + 1))

        x_v = x.rearrange("b (t p) d -> p (b t) d", p=P)
        out_v = out.rearrange("b (t p) d -> p (b t) d", p=P)
        ada_v = ada_w.rearrange("o (p k) n -> p (o k) n", k=KT)
        w_in_v = w_in.rearrange("o (k p) n -> p (o k) n", p=P)
        w_out_v = w_out.rearrange("o (h k p) n -> p (o h) k n", k=2, p=P)
        w_raw_k = w_raw[:, :, :].rearrange("p s (k n) -> p s k n", k=KT)
        h_hi_v = h_hi[:, :, :].rearrange("p k (s t) -> p k s t", s=2)
        h_lo_v = h_lo[:, :, :].rearrange("p k (s t) -> p k s t", s=2)

        y_v = y[:, :, :].rearrange("p (s c) d -> p s c d", s=2)

        n_dram = nc.dram_tensor("n_dram", (P, NCH, P), F32).ap()
        t_dram = nc.dram_tensor("t_dram", (P, NCH, P), F32).ap()
        u_dram = nc.dram_tensor("u_dram", (P, NCH, P), F32).ap()

        block = ctx.enter_context(nc.Block())

        @block.sync
        def _(sp):
            def load_tile(u, k):
                head = u // 2
                slot = k % 2
                if k < PIECES:
                    off = {0: 2048 + head * DV, 1: 2048 + P + head * DV, 2: head * DK, 3: 1024 + head * DK,
                           4: Z_OFF + head * DV, 5: Z_OFF + P + head * DV}[k]
                    src, dst = w_in_v[:, :, bass.ds(off, P)], w_raw_k[:, slot, :, :]
                else:
                    src, dst = w_out_v[:, head, k - PIECES, :], w_raw[:, slot, :]
                sp.dma_start(dst, src).then_inc(raw_in[slot], 16)

            def next_tile(u, k):
                passed(sp, "w_lo_done", u, k - 1)
                load_tile(u, k)

            def diagonal(m, c):
                return bass.AP(m.tensor, c * P, [[BLK * (NCH * P + 1), NBLK], [NCH * P, BLK], [1, BLK]])

            sp.dma_start(rows[:, 0, :], conv_w.rearrange("o j (t p) -> (o j t) p", p=P)).then_inc(rows_in, 16)
            sp.dma_start(rows[0:24, 1, :], ada_b.rearrange("o (t p) -> (o t) p", p=P)).then_inc(rows_in, 16)
            sp.dma_start(rows[24:32, 1, :], norm_w.rearrange("o (t p) -> (o t) p", p=P)).then_inc(rows_in, 16)
            sp.dma_start(rows[32:34, 1, :], gdn_norm_w.rearrange("o (t p) -> (o t) p", p=P)).then_inc(rows_in, 16)
            sp.dma_start(c_col[:, :], c.rearrange("o (p k) -> p (o k)", k=KT)).then_inc(c_in, 16)
            sp.dma_start(y[:, 0:4, :], x_v[:, 0:4, :]).then_inc(x_in[0], 16)
            load_tile(0, 0)
            for k in range(KT):
                if k == 4:
                    sp.wait_ge(rows_turned, 1)
                    load_tile(0, 1)
                if k >= 2:
                    sp.wait_ge(ada_summed, k - 1)
                sp.dma_start(ada_buf[:, k % 2, :], ada_v[:, k, 0:2 * D_MODEL]).then_inc(ada_in[k % 2], 16)
            sp.wait_ge(consts, 2)
            sp.dma_start(t_dram, t16[:, :, :]).then_inc(tu_stored, 16)
            sp.dma_start(u_dram, u16[:, :, :]).then_inc(tu_stored, 16)
            sp.dma_start(y[:, 4:8, :], x_v[:, 4:8, :]).then_inc(x_in[1], 16)
            sp.dma_start(wba_raw, w_in_v[:, :, BA_OFF:BA_OFF + 16]).then_inc(wba_in, 16)
            sp.dma_start(small[:, 0:8], a_log.partition_broadcast(P)).then_inc(bias_in, 16)
            sp.dma_start(small[:, 8:16], dt_bias.partition_broadcast(P)).then_inc(bias_in, 16)
            sp.dma_start(gate_bc[:, :], ada_b[0:1, 2 * D_MODEL:].partition_broadcast(P)).then_inc(bias_in, 16)
            next_tile(0, 2)
            next_tile(0, 3)
            for k in range(KT):
                if k == 0:
                    sp.wait_ge(mod_mm, 1)
                if k >= 2:
                    sp.wait_ge(ada_summed, KT + k - 1)
                sp.dma_start(gate_buf[:, k % 2, :], ada_v[:, k, 2 * D_MODEL:]).then_inc(ada_in[k % 2], 16)

            for k in (4, 5):
                next_tile(0, k)

            def phase_b(u, last=False):
                for k in (6, 7):
                    next_tile(u, k)
                passed(sp, "n_done", u, 2)
                sp.dma_start(n_dram, nmat).then_inc(n_stored, 16)
                sp.wait_ge(n_stored, 16 * (u + 1))
                for c in range(NCH):
                    sp.dma_start(blk_n[c * NBLK:(c + 1) * NBLK, :, :], diagonal(n_dram, c)).then_inc(blk_in, 16)
                if not last:
                    next_tile(u + 1, 0)
                passed(sp, "base_done", u, 1)
                for dst, src in ((t_dram, blk_y), (u_dram, blk_yt)):
                    for c in range(NCH):
                        sp.dma_start(diagonal(dst, c), src[c * NBLK:(c + 1) * NBLK, :, :]).then_inc(tu_stored, 16)
                sp.wait_ge(tu_stored, 16 * (2 + 2 * NCH * (u + 1)))
                sp.dma_start(t16[:, :, :], t_dram).then_inc(blk_back, 16)
                sp.dma_start(u16[:, :, :], u_dram).then_inc(blk_back, 16)
                if not last:
                    next_tile(u + 1, 1)

            with sp.Fori(0, UNITS - 1) as u:
                phase_b(u)
                for k in (2, 3, 4, 5):
                    next_tile(u + 1, k)
            phase_b(UNITS - 1, last=True)

            passed(sp, "w_lo_done", UNITS - 1, 8)
            sp.dma_start(w_raw[:, 0, :], final_norm_w.rearrange("(o n) -> o n", o=1).partition_broadcast(P)
                         ).then_inc(fw_in, 16)
            for t in range(TILES):
                sp.wait_ge(fin_done, t + 1)
                sp.dma_start(out_v[:, t, :], fin[:, t % 2, :]).then_inc(stored[t % 2], 16)
            for i in range(2):
                sp.wait_ge(stored[i], 16 * TILES // 2)

        @block.tensor
        def _(pe):
            prime(pe, "tensor")

            def project(u, first, last):
                for n in range(first, last):
                    m, r = divmod(n, MM)
                    k, part_no = divmod(r, 3)
                    if r == 0:
                        passed(pe, "w_lo_done", u, m + 1)
                        passed(pe, "evacuated", u, m - 1)
                    w, h = ((w_hi, h_hi_v), (w_hi, h_lo_v), (w_lo, h_hi_v))[part_no]
                    mm = nc.tensor.matmul(bank[m % 2][:, :], w[:, m % 2, k, :], h[:, k, u % 2, :],
                                          start=(r == 0), stop=(r == MM - 1))
                    if r == MM - 1:
                        mm.then_inc(S["projected"], 1)

            def turn_o(g, c):
                passed(pe, "o_scaled", g, c + 1)
                passed(pe, "qs_scaled", g, min(c + 2, 4))
                for m in range(2):
                    mm = nc.tensor.transpose(bank[3][:, m * P:(m + 1) * P], o_n[:, m * P:(m + 1) * P], ident[:, :])
                mm.then_inc(S["o_turned"], 1)

            def out_project(g, c):
                if c == 0:
                    passed(pe, "w_lo_done", g, 8)
                    passed(pe, "attn_out", g, 1)
                passed(pe, "og_lo_done", g, c + 1)
                passed(pe, "y_added", g, c)
                for n in range(2):
                    for m in range(2):
                        for q, (a, w) in enumerate(((og_hi, wo_hi), (og_hi, wo_lo), (og_lo, wo_hi))):
                            mm = nc.tensor.matmul(bank[6 + n][:, :], a[:, m, :], w[:, m, n * 512:(n + 1) * 512],
                                                  start=(m == 0 and q == 0), stop=(m == 1 and q == 2))
                mm.then_inc(S["out_done"], 1)

            def phase_a(u, g, first=18):
                pos = [first]

                def fill(n):
                    if u is not None:
                        project(u, pos[0], pos[0] + n)
                        pos[0] += n

                for c in range(NCH):
                    passed(pe, "state_done", g, c + 1)
                    passed(pe, "o_done", g, c)
                    nc.tensor.matmul(bank[2][:, 0:DV], kq[:, c, 0:DK], state[:, :], start=True, stop=True
                                     ).then_inc(S["ks_done"], 1)
                    passed(pe, "og_done", g, max(c - 1, 0))
                    nc.tensor.matmul(bank[3][:, 0:DV], kq[:, c, DK:2 * DK], state[:, :], start=True, stop=True
                                     ).then_inc(S["qs_done"], 1)
                    fill(6)
                    if c == 0:
                        passed(pe, "merge_d_out", g, 3)
                    else:
                        passed(pe, "x_out", g, c)
                    passed(pe, "r_done", g, c + 1)
                    nc.tensor.matmul(bank[4][:, 0:DV], u_fin[:, c, :], r_rhs, start=True, stop=True
                                     ).then_inc(S["x_done"], 1)
                    fill(6)
                    passed(pe, "x_out", g, c + 1)
                    nc.tensor.matmul(bank[5][:, 0:DV], kdec[:, c, :], xs, start=True, stop=True
                                     ).then_inc(S["kv_done"], 1)
                    if c == 0:
                        passed(pe, "attn_out", g, 1)
                    nc.tensor.matmul(bank[2][:, 0:DV], attn_t[:, c, :], xs, start=True, stop=True
                                     ).then_inc(S["av_done"], 1)
                    if c > 0:
                        turn_o(g, c - 1)
                    fill(6)
                    if c > 0:
                        out_project(g, c - 1)
                fill(3)
                turn_o(g, NCH - 1)
                fill(3)
                out_project(g, NCH - 1)

            def phase_b(u, last=False):
                project(u, 96, 108)
                passed(pe, "silu_done", u, 4)
                for c in range(NCH):
                    if c == 0:
                        passed(pe, "o_done", u, 0)
                    elif c == 1:
                        passed(pe, "og_done", u, 0)
                    else:
                        passed(pe, "turned_out", u, c - 1)
                    for i, src in enumerate((kq[:, c, 0:DK], kq[:, c, DK:2 * DK],
                                             cv[:, 0, c * P:(c + 1) * P], cv[:, 1, c * P:(c + 1) * P])):
                        mm = nc.tensor.transpose(bank[2 + c % 2][:, i * P:(i + 1) * P], src, ident[:, :])
                    mm.then_inc(S["turned"], 1)
                project(u, 108, 114)
                passed(pe, "g_after_done", u, 1)
                passed(pe, "x_out", u, 0)
                nc.tensor.matmul(bank[4][:, :], upto[:, :], g_after.rearrange("p c t -> p (c t)"),
                                 start=True, stop=True).then_inc(S["decay_mm"], 1)
                passed(pe, "state_done", u, 0)
                for c in range(NCH):
                    if c == 2:
                        passed(pe, "y_added", u, 0)
                    b = bank[5 + c // 2]
                    o = (c % 2) * 2 * P
                    nc.tensor.matmul(b[:, o:o + P], kq[:, c, 0:DK], kq[:, c, 0:DK], start=True, stop=True)
                    mm = nc.tensor.matmul(b[:, o + P:o + 2 * P], kq[:, c, DK:2 * DK], kq[:, c, 0:DK],
                                          start=True, stop=True)
                    if c % 2 == 1:
                        mm.then_inc(S["gram_done"], 1)
                project(u, 114, 120)
                passed(pe, "attn_done", u, 2)
                for c in range(NCH):
                    mm = nc.tensor.transpose(bank[7][:, c * P:(c + 1) * P], attn[:, c, :], ident[:, :])
                mm.then_inc(S["attn_turned"], 1)
                project(u, 120, 132)
                pe.wait_ge(blk_back, 32 * (u + 1))
                passed(pe, "turned_out", u, 4)
                passed(pe, "decay_exp", u, 1)
                banks = ((2, 3, 4), (5, 6, 2), (3, None, 4))
                for lv in range(3):
                    bp, bt, bu = banks[lv]
                    t_s, u_s = (t16, u16) if lv == 0 else (tm, um)
                    if lv > 0:
                        passed(pe, "merge_d_out", u, lv)
                    for c in range(NCH):
                        mm = nc.tensor.matmul(bank[bp][:, c * P:(c + 1) * P], nmat[:, c, :], u_s[:, c, :],
                                              start=True, stop=True)
                    mm.then_inc(S["merge_p"], 1)
                    if lv < 2:
                        project(u, 132 + 6 * lv, 138 + 6 * lv)
                    elif not last:
                        project(u + 1, 9, 18)
                    passed(pe, "merge_p_out", u, lv + 1)
                    for c in range(NCH):
                        if bt is not None:
                            nc.tensor.matmul(bank[bt][:, c * P:(c + 1) * P], pmat[:, c, :], t_s[:, c, :],
                                             start=True, stop=True)
                    for c in range(NCH):
                        mm = nc.tensor.matmul(bank[bu][:, c * P:(c + 1) * P], t_s[:, c, :], pmat[:, c, :],
                                              start=True, stop=True)
                    mm.then_inc(S["merge_d"], 1)
                    if lv == 1 and not last:
                        project(u + 1, 0, 9)

            pe.wait_ge(rows_in, 64)
            pe.wait_ge(consts, 1)
            nc.tensor.transpose(bank[7][:, 0:P], rows[:, 0, :], ident[:, :])
            nc.tensor.transpose(bank[7][:, P:P + 34], rows[0:34, 1, :], ident[0:34, 0:34]).then_inc(rows_turned, 1)

            def turn_x(half, first, last):
                for k in range(first, last):
                    if half == 1 or k >= 4:
                        pe.wait_ge(h_done, 8 * half + k - 3)
                    for t in range(4):
                        mm = nc.tensor.transpose(bank[2 + k % 4][:, t * P:(t + 1) * P],
                                                 xn[:, t, k * P:(k + 1) * P], ident[:, :])
                    mm.then_inc(x_turned, 1)

            pe.wait_ge(xn_done, 4)
            turn_x(0, 0, 4)
            pe.wait_ge(ada_summed, KT)
            for j in range(16):
                mm = nc.tensor.matmul(bank[6][:, j:j + 1], ada_acc[:, j * P:(j + 1) * P], ones[:, 0:1],
                                      start=True, stop=True)
            mm.then_inc(mod_mm, 1)
            turn_x(0, 4, KT)
            pe.wait_ge(h_split, KT)
            project(0, 0, 24)
            pe.wait_ge(xn_done, 8)
            turn_x(1, 0, KT)
            project(0, 24, 48)
            pe.wait_ge(wba_split, 2)
            pe.wait_ge(h_split, 2 * KT)
            pe.wait_ge(mod_done, 2)
            for t in range(TILES):
                for k in range(KT):
                    for q, (h, w) in enumerate(((h_hi, wba_hi), (h_lo, wba_hi), (h_hi, wba_lo))):
                        mm = nc.tensor.matmul(bank[6][:, t * 16:(t + 1) * 16], h[:, k, t * P:(t + 1) * P],
                                              w[:, k, :], start=(k == 0 and q == 0), stop=(k == KT - 1 and q == 2))
            mm.then_inc(ba_mm, 1)
            project(0, 48, 72)
            pe.wait_ge(ada_summed, 2 * KT)
            pe.wait_ge(h_done, 2 * KT)
            for n in range(2):
                mm = nc.tensor.matmul(bank[2 + n][:, :], ones[:, :],
                                      ada_acc[:, 2 * D_MODEL + n * 512:2 * D_MODEL + (n + 1) * 512],
                                      start=True, stop=True)
            mm.then_inc(gate_mm, 1)
            pe.wait_ge(g_step, 4)
            gt = g_tab[:, :, :].rearrange("p u c -> p (u c)")
            for i, m in enumerate((upto, after, ones)):
                mm = nc.tensor.matmul(bank[4][:, i * 64:(i + 1) * 64], m[:, :], gt, start=True, stop=True)
            mm.then_inc(sums_mm, 1)
            project(0, 72, 96)
            pe.wait_ge(tables_done, 3)
            pe.wait_ge(gate_done, 2)
            with pe.Fori(0, UNITS - 1) as u:
                phase_b(u)
                phase_a(u + 1, u)
            phase_b(UNITS - 1, last=True)
            phase_a(None, UNITS - 1)

        @block.scalar
        def _(act):
            prime(act, "scalar")

            def split_hi(u, k):
                tile_landed(act, u, k)
                if k < PIECES:
                    passed(act, "projected", u, k - 1)
                    dst, src = w_hi[:, k % 2, :, :], w_raw_k[:, k % 2, :, :]
                else:
                    passed(act, "w_gated", u, k - 5)
                    passed(act, "out_done", u, 0)
                    dst, src = wo_hi[:, k - PIECES, :], w_raw[:, k % 2, :]
                nc.scalar.activation(dst, src, ACT.Copy).then_inc(S["w_hi_done"], 1)

            def evacuate(u, m):
                passed(act, "projected", u, m + 1)
                if m < CONVED:
                    passed(act, "conv_done", u, m - 1)
                    nc.scalar.activation(pre[:, m % 2, 3:3 + HALF], bank[m % 2][:, :], ACT.Copy
                                         ).then_inc(S["evacuated"], 1)
                else:
                    passed(act, "silu_done", u, m - 3)
                    nc.scalar.activation(th[:, m - 4, :], bank[m % 2][:, :], ACT.Tanh, scale=0.5
                                         ).then_inc(S["tanh_done"], 1)
                    passed(act, "og_done", u, 0)
                    nc.scalar.activation(zt[:, m - 4, :], bank[m % 2][:, :], ACT.Copy
                                         ).then_inc(S["evacuated"], 1)

            def tanh(u, m):
                passed(act, "conv_done", u, m + 1)
                passed(act, "silu_done", u, m - 1 if m < 2 else m - 5)
                nc.scalar.activation(th[:, m, :], cv[:, m, :], ACT.Tanh, scale=0.5
                                     ).then_inc(S["tanh_done"], 1)

            def og_high(g, c):
                passed(act, "og_done", g, c + 1)
                passed(act, "out_done", g, c)
                nc.scalar.activation(og_hi[:, :, :], og, ACT.Copy).then_inc(S["og_hi_done"], 1)

            def phase_a(u, g):
                for c in range(NCH):
                    passed(act, "qs_done", g, c + 1)
                    passed(act, "o_done", g, c)
                    nc.scalar.activation(qss, bank[3][:, 0:DV], ACT.Identity, scale=e_gc[:, g, c:c + 1]
                                         ).then_inc(S["qs_scaled"], 1)
                    if u is not None and c > 0:
                        evacuate(u, c - 1)
                    passed(act, "x_done", g, c + 1)
                    passed(act, "av_done", g, c)
                    nc.scalar.activation(xs, bank[4][:, 0:DV], ACT.Copy).then_inc(S["x_out"], 1)
                    if u is not None:
                        split_hi(u, c + 1)
                        if c > 0:
                            tanh(u, c - 1)
                    if c > 0:
                        og_high(g, c - 1)
                    passed(act, "o_done", g, c + 1)
                    passed(act, "o_mean", g, c)
                    passed(act, "o_squared", g, c)
                    nc.scalar.activation(junk, o_raw, ACT.Square, accum_out=oss[:, 0:1]
                                         ).then_inc(S["o_squared"], 1)
                og_high(g, NCH - 1)
                if u is not None:
                    evacuate(u, 3)
                    tanh(u, 3)

            def phase_b(u, last=False):
                split_hi(u, 5)
                for c in range(NCH):
                    passed(act, "turned", u, c + 1)
                    if c == 0:
                        passed(act, "norms_done", u, 0)
                    passed(act, "squared", u, 2 * c)
                    nc.scalar.activation(junk_b[:, :], bank[2 + c % 2][:, 0:P], ACT.Square,
                                         accum_out=st[:, c:c + 1]).then_inc(S["squared"], 1)
                    passed(act, "squared", u, 2 * c + 1)
                    nc.scalar.activation(junk_b[:, :], bank[2 + c % 2][:, P:2 * P], ACT.Square,
                                         accum_out=st[:, NCH + c:NCH + c + 1]).then_inc(S["squared"], 1)
                    if c == 1:
                        split_hi(u, 6)
                passed(act, "decay_mm", u, 1)
                nc.scalar.activation(decay.rearrange("p c t -> p (c t)"), bank[4][:, :], ACT.Exp
                                     ).then_inc(S["decay_exp"], 1)
                split_hi(u, 7)
                passed(act, "attn_turned", u, 1)
                nc.scalar.activation(attn_t.rearrange("p c t -> p (c t)"), bank[7][:, :], ACT.Copy
                                     ).then_inc(S["attn_out"], 1)
                evacuate(u, 4)
                if not last:
                    split_hi(u + 1, 0)
                evacuate(u, 5)

            act.wait_ge(c_in, 16)
            nc.scalar.activation(c_th[:, :], c_col[:, :], ACT.Tanh, scale=0.5).then_inc(c_step, 1)

            def square_x(half):
                act.wait_ge(x_in[half], 16)
                for t in range(4 * half, 4 * half + 4):
                    if t > 0:
                        act.wait_ge(x_squared, t)
                    nc.scalar.activation(hf.rearrange("p s t -> p (s t)"), y[:, t, :], ACT.Square,
                                         accum_out=xss[:, t:t + 1]).then_inc(x_squared, 1)

            def evacuate_h(half, first, last):
                for k in range(first, last):
                    n = 8 * half + k
                    act.wait_ge(x_turned, n + 1)
                    if n >= 2:
                        act.wait_ge(h_split, n - 1)
                    nc.scalar.activation(hf[:, k % 2, :], bank[2 + k % 4][:, :], ACT.Identity,
                                         bias=mod[:, k:k + 1], scale=mod[:, 8 + k:9 + k]).then_inc(h_done, 1)

            square_x(0)
            split_hi(0, 0)
            act.wait_ge(mod_done, 2)
            evacuate_h(0, 0, KT)
            split_hi(0, 1)
            act.wait_ge(h_split, KT)
            square_x(1)
            evacuate(0, 0)
            evacuate_h(1, 0, KT)
            split_hi(0, 2)
            tanh(0, 0)
            act.wait_ge(wba_in, 16)
            nc.scalar.activation(wba_hi, wba_raw, ACT.Copy).then_inc(wba_split, 1)
            evacuate(0, 1)
            split_hi(0, 3)
            tanh(0, 1)
            ba = bank[6][:, 0:P].rearrange("p (c h) -> p h c", h=16)
            act.wait_ge(ba_mm, 1)
            nc.scalar.activation(beta[:, :, :].rearrange("p (h s) c -> p h (s c)", s=2), ba[:, 0:8, :],
                                 ACT.Exp, scale=-1.0).then_inc(beta_step, 1)
            act.wait_ge(bias_in, 48)
            nc.scalar.activation(small[:, 16:24], small[:, 0:8], ACT.Exp).then_inc(g_exp, 1)
            act.wait_ge(g_step, 2)
            nc.scalar.activation(e_gc[:, :, :], e_kd[:, :, :], ACT.Exp, scale=-1.0).then_inc(g_exp, 1)
            act.wait_ge(g_exp, 2)
            nc.scalar.activation(e_gl[:, :, :], e_gc[:, :, :], ACT.Ln, bias=1.0).then_inc(g_exp, 1)
            evacuate(0, 2)
            split_hi(0, 4)
            tanh(0, 2)
            act.wait_ge(sums_mm, 1)
            for i, tab in enumerate((e_gc, e_kd, e_gl)):
                act.wait_ge(g_step, 4)
                nc.scalar.activation(tab[:, :, :].rearrange("p u c -> p (u c)"), bank[4][:, i * 64:(i + 1) * 64],
                                     ACT.Exp).then_inc(tables_done, 1)
            evacuate(0, 3)
            tanh(0, 3)
            with act.Fori(0, UNITS - 1) as u:
                phase_b(u)
                phase_a(u + 1, u)
            phase_b(UNITS - 1, last=True)
            phase_a(None, UNITS - 1)
            for t in range(TILES):
                passed(act, "y_added", UNITS - 1, 4 if t >= 4 else 0)
                if t > 0:
                    act.wait_ge(fin_squared, t)
                nc.scalar.activation(w_raw[:, 1, :], y[:, t, :], ACT.Square, accum_out=fss[:, t:t + 1]
                                     ).then_inc(fin_squared, 1)

        @block.vector
        def _(dve):
            prime(dve, "vector")
            stt = nc.vector.scalar_tensor_tensor

            def convolve(u, m):
                head = u // 2
                tile = (16 + 2 * head, 17 + 2 * head, head, 8 + head)[m]
                r = m % 2
                passed(dve, "evacuated", u, m + 1)
                if m < 2:
                    passed(dve, "turned", u, 0)
                for j in range(TAPS):
                    tap = cw[:, bass.ds(tile + 32 * j, 1)]
                    if j == 0:
                        i = nc.vector.tensor_scalar(cv[:, m, :], pre[:, r, 0:HALF], tap, None, ALU.mult)
                    else:
                        passed(dve, "conv_step", u, 4 * m + j)
                        i = stt(out=cv[:, m, :], in0=pre[:, r, j:j + HALF], scalar=tap, in1=cv[:, m, :],
                                op0=ALU.mult, op1=ALU.add)
                    i.then_inc(S["conv_step"], 1)
                nc.vector.tensor_scalar(tails[:, m, 0:3], pre[:, r, HALF:HALF + 3], even[:, bass.ds(u, 1)],
                                        None, ALU.mult)
                passed(dve, "conv_step", u, 4 * m + 4)
                nc.vector.tensor_copy(pre[:, r, 0:3], tails[:, (m + 2) % 4, 0:3]).then_inc(S["conv_done"], 1)

            def silu(u, m):
                passed(dve, "tanh_done", u, m + 1)
                if m < 2:
                    dst = a = cv[:, m, :]
                    t = th[:, m, :]
                elif m < 4:
                    if m == 2:
                        passed(dve, "qs_done", u, 0)
                    o = DK if m == 2 else 0
                    dst = kq[:, :, o:o + DK]
                    a = cv[:, m, :].rearrange("p (c t) -> p c t", c=NCH)
                    t = th[:, m, :].rearrange("p (c t) -> p c t", c=NCH)
                else:
                    passed(dve, "evacuated", u, m + 1)
                    dst = a = zt[:, m - 4, :]
                    t = th[:, m - 4, :]
                stt(out=dst, in0=t, scalar=1.0, in1=a, op0=ALU.add, op1=ALU.mult).then_inc(S["silu_done"], 1)

            def gate_tile(u, k):
                tile_landed(dve, u, k)
                nc.vector.tensor_tensor(w_raw[:, k % 2, :], w_raw[:, k % 2, :], gate_bc[:, :], ALU.mult
                                        ).then_inc(S["w_gated"], 1)

            def norm_o(g, c):
                passed(dve, "o_pow", g, c + 1)
                passed(dve, "o_turned", g, c)
                nc.vector.tensor_scalar(o_n, o_raw, oss[:, 2:3], sc[:, 4, c:c + 1], ALU.mult, ALU.mult
                                        ).then_inc(S["o_scaled"], 1)

            def gate_o(g, c):
                passed(dve, "o_turned", g, c + 1)
                passed(dve, "og_lo_done", g, c)
                if c == 0:
                    passed(dve, "silu_done", g, 6)
                for m in range(2):
                    i = stt(out=og[:, m, :], in0=bank[3][:, m * P:(m + 1) * P], scalar=small[:, 32 + m:33 + m],
                            in1=zt[:, m, c * P:(c + 1) * P], op0=ALU.mult, op1=ALU.mult)
                i.then_inc(S["og_done"], 1)

            def add_y(g, c):
                passed(dve, "out_done", g, c + 1)
                for n in range(2):
                    yt = y_v[:, g % 2, c, n * 512:(n + 1) * 512]
                    i = nc.vector.tensor_tensor(yt, bank[6 + n][:, :], yt, ALU.add)
                i.then_inc(S["y_added"], 1)

            def phase_a(u, g):
                passed(dve, "qs_done", g, 0)
                nc.vector.tensor_scalar(state[:, :], state[:, :], odd[:, bass.ds(g, 1)], None, ALU.mult
                                        ).then_inc(S["state_done"], 1)
                for c in range(NCH):
                    passed(dve, "ks_done", g, c + 1)
                    passed(dve, "v_scaled", g, c + 1)
                    passed(dve, "x_done", g, c)
                    stt(out=r_rhs, in0=bank[2][:, 0:DV], scalar=sc[:, 1, c:c + 1], in1=vt[:, c, :],
                        op0=ALU.mult, op1=ALU.add).then_inc(S["r_done"], 1)
                    if c > 0:
                        norm_o(g, c - 1)
                    if c > 1:
                        add_y(g, c - 2)
                    if u is not None and c > 0:
                        convolve(u, c - 1)
                    passed(dve, "kv_done", g, c + 1)
                    passed(dve, "qs_done", g, c + 1)
                    stt(out=state[:, :], in0=state[:, :], scalar=e_gl[:, g, c:c + 1], in1=bank[5][:, 0:DV],
                        op0=ALU.mult, op1=ALU.add).then_inc(S["state_done"], 1)
                    passed(dve, "av_done", g, c + 1)
                    passed(dve, "qs_scaled", g, c + 1)
                    passed(dve, "o_scaled", g, c)
                    nc.vector.tensor_tensor(o_raw, bank[2][:, 0:DV], qss, ALU.add).then_inc(S["o_done"], 1)
                    if c > 0:
                        gate_o(g, c - 1)
                    passed(dve, "o_squared", g, c + 1)
                    nc.vector.tensor_scalar(oss[:, 1:2], oss[:, 0:1], sc[:, 5, c:c + 1], NORM_EPS,
                                            ALU.mult, ALU.add).then_inc(S["o_mean"], 1)
                    if u is not None and c > 1:
                        silu(u, c - 2)
                norm_o(g, 3)
                add_y(g, 2)
                gate_o(g, 3)
                if u is not None:
                    convolve(u, 3)
                add_y(g, 3)

            def phase_b(u, last=False):
                silu(u, 2)
                silu(u, 3)
                gate_tile(u, 6)
                for c in range(NCH):
                    passed(dve, "turned", u, c + 1)
                    passed(dve, "squared", u, 2 * c + 2)
                    if c == 0:
                        passed(dve, "kv_done", u, 0)
                    nc.vector.tensor_scalar(kdec[:, c, :], bank[2 + c % 2][:, 0:P], e_kd[:, u, c:c + 1], None,
                                            ALU.mult)
                    nc.vector.tensor_copy(vt[:, c, :], bank[2 + c % 2][:, 2 * P:4 * P]
                                          ).then_inc(S["turned_out"], 1)
                passed(dve, "norms_done", u, 1)
                rk, rq = rs[:, 0:NCH], rs[:, NCH:2 * NCH]
                nc.vector.tensor_tensor(sc[:, 0, :], beta[:, u, :], rk, ALU.mult).then_inc(S["scalar_step"], 1)
                nc.vector.tensor_scalar(sc[:, 4, :], rq, DK ** -0.5, None, ALU.mult).then_inc(S["scalar_step"], 1)
                passed(dve, "scalar_step", u, 2)
                nc.vector.tensor_tensor(sc[:, 3, :], sc[:, 0, :], rk, ALU.mult).then_inc(S["scalar_step"], 1)
                nc.vector.tensor_scalar(sc[:, 2, :], sc[:, 0, :], 0.5, None, ALU.mult).then_inc(S["scalar_step"], 1)
                stt(out=sc[:, 5, :], in0=sc[:, 4, :], scalar=1.0 / DV, in1=sc[:, 4, :], op0=ALU.mult, op1=ALU.mult)
                passed(dve, "scalar_step", u, 3)
                stt(out=sc[:, 1, :], in0=sc[:, 3, :], scalar=-1.0, in1=e_gc[:, u, :], op0=ALU.mult, op1=ALU.mult
                    ).then_inc(S["scalars_done"], 1)
                passed(dve, "scalars_done", u, 1)
                passed(dve, "decay_done", u, 1)
                for p in range(2):
                    passed(dve, "gram_done", u, p + 1)
                    b = bank[5 + p][:, :].rearrange("p (c w t) -> p c w t", c=2, w=2)
                    for c in (2 * p, 2 * p + 1):
                        i = stt(out=nmat[:, c, :], in0=b[:, c % 2, 0, :], scalar=sc[:, 3, c:c + 1],
                                in1=decay[:, c, :], op0=ALU.mult, op1=ALU.mult)
                    i.then_inc(S["n_done"], 1)
                    nc.vector.tensor_tensor(attn[:, 2 * p:2 * p + 2, :], b[:, :, 1, :],
                                            decay[:, 2 * p:2 * p + 2, :], ALU.mult).then_inc(S["attn_done"], 1)
                gate_tile(u, 7)
                dve.wait_ge(blk_in, 16 * NCH * (u + 1))
                nc.vector.tensor_copy(blk_y[:, :, :], blk_id[:, :, :]).then_inc(S["base_step"], 1)
                passed(dve, "base_step", u, 1)
                for j in range(BLK - 1):
                    rows_, cols = BLK - 1 - j, j + 1
                    shape = [NBLK * NCH, rows_, cols]
                    tmp = blk_tmp[:, j + 1:, 0:cols]
                    nc.vector.tensor_tensor(tmp, blk_n[:, j + 1:, j:j + 1].to_broadcast(shape),
                                            blk_y[:, j:j + 1, 0:cols].to_broadcast(shape), ALU.mult
                                            ).then_inc(S["base_step"], 1)
                    passed(dve, "base_step", u, 2 * j + 2)
                    nc.vector.tensor_tensor(blk_y[:, j + 1:, 0:cols], blk_y[:, j + 1:, 0:cols], tmp,
                                            ALU.subtract).then_inc(S["base_step"], 1)
                    passed(dve, "base_step", u, 2 * j + 3)
                nc.vector.tensor_copy(blk_yt, blk_y.rearrange("p i j -> p j i")
                                      ).then_inc(S["base_done"], 1)
                silu(u, 4)
                banks = ((2, 3, 4), (5, 6, 2), (3, None, 4))
                for lv in range(3):
                    bp, bt, bu = banks[lv]
                    t_s, u_s = (t16[:, :, :], u16[:, :, :]) if lv == 0 else (tm, um)
                    passed(dve, "merge_p", u, lv + 1)
                    nc.vector.tensor_tensor(pmat, bank[bp][:, :].rearrange("p (c t) -> p c t", c=NCH),
                                            pair_mask[:, lv:lv + 1, :].to_broadcast([P, NCH, P]), ALU.mult
                                            ).then_inc(S["merge_p_out"], 1)
                    if lv == 1:
                        silu(u, 5)
                    passed(dve, "merge_d", u, lv + 1)
                    if bt is not None:
                        nc.vector.tensor_tensor(tm, t_s, bank[bt][:, :].rearrange("p (c t) -> p c t", c=NCH),
                                                ALU.subtract)
                    nc.vector.tensor_tensor(um if lv < 2 else u_fin, u_s,
                                            bank[bu][:, :].rearrange("p (c t) -> p c t", c=NCH),
                                            ALU.subtract).then_inc(S["merge_d_out"], 1)

            def norm_x(half):
                dve.wait_ge(x_pow, half + 1)
                if half == 1:
                    dve.wait_ge(x_turned, KT)
                for t in range(4):
                    nc.vector.tensor_scalar(xn[:, t, :], y[:, 4 * half + t, :],
                                            xrs[:, 4 * half + t:4 * half + t + 1], None, ALU.mult
                                            ).then_inc(xn_done, 1)

            def sum_ada(k, lo, hi, base):
                dve.wait_ge(ada_in[k % 2], 16 * (base // 2 + k // 2 + 1))
                src = (ada_buf if lo == 0 else gate_buf)[:, k % 2, :]
                if k == 0:
                    i = nc.vector.tensor_scalar(ada_acc[:, lo:hi], src, c_th[:, 0:1], None, ALU.mult)
                else:
                    dve.wait_ge(ada_summed, base + k)
                    i = stt(out=ada_acc[:, lo:hi], in0=src, scalar=c_th[:, k:k + 1], in1=ada_acc[:, lo:hi],
                            op0=ALU.mult, op1=ALU.add)
                i.then_inc(ada_summed, 1)

            def split_h(half, first, last):
                for k in range(first, last):
                    n = 8 * half + k
                    dve.wait_ge(h_done, n + 1)
                    nc.vector.tensor_copy(h_hi_v[:, k, half, :], hf[:, k % 2, :]).then_inc(hi_step, 1)
                    dve.wait_ge(hi_step, n + 1)
                    nc.vector.tensor_tensor(h_lo_v[:, k, half, :], hf[:, k % 2, :],
                                            h_hi_v[:, k, half, :].bitcast(F32), ALU.subtract
                                            ).then_inc(h_split, 1)

            dve.wait_ge(rows_turned, 1)
            nc.vector.tensor_copy(cw[:, :], bank[7][:, 0:P])
            nc.vector.tensor_copy(rows_t[:, :], bank[7][:, P:P + 34]).then_inc(rows_out, 1)
            dve.wait_ge(rows_out, 1)
            nc.vector.tensor_scalar(small[:, 32:34], rows_t[:, 32:34], 0.5, None, ALU.mult).then_inc(rows_out, 1)
            dve.wait_ge(c_step, 1)
            stt(out=c_th[:, :], in0=c_th[:, :], scalar=1.0, in1=c_col[:, :], op0=ALU.add, op1=ALU.mult
                ).then_inc(c_step, 1)
            dve.wait_ge(c_step, 2)
            nc.vector.tensor_scalar(c_th[:, :], c_th[:, :], 0.5, None, ALU.mult).then_inc(c_step, 1)
            dve.wait_ge(c_step, 3)
            norm_x(0)
            for k in range(KT):
                sum_ada(k, 0, 2 * D_MODEL, 0)
            dve.wait_ge(mod_mm, 1)
            nc.vector.tensor_tensor(mod[:, 0:16], bank[6][:, 0:16], rows_t[:, 0:16], ALU.add).then_inc(mod_done, 1)
            dve.wait_ge(mod_done, 1)
            stt(out=mod[:, 8:16], in0=mod[:, 8:16], scalar=1.0, in1=rows_t[:, 24:32], op0=ALU.add, op1=ALU.mult
                ).then_inc(mod_done, 1)
            split_h(0, 0, KT)
            norm_x(1)
            convolve(0, 0)
            split_h(1, 0, KT)
            silu(0, 0)
            dve.wait_ge(wba_split, 1)
            nc.vector.tensor_tensor(wba_lo, wba_raw, wba_hi.bitcast(F32), ALU.subtract
                                    ).then_inc(wba_split, 1)
            convolve(0, 1)
            silu(0, 1)
            dve.wait_ge(beta_step, 1)
            nc.vector.tensor_scalar(beta[:, :, :], beta[:, :, :], 1.0, None, ALU.add).then_inc(beta_step, 1)
            dve.wait_ge(beta_step, 2)
            nc.vector.reciprocal(beta[:, :, :], beta[:, :, :]).then_inc(beta_step, 1)
            dve.wait_ge(bias_in, 48)
            heads = "p (h s) c -> p h (s c)"
            g_v = g_tab[:, :, :].rearrange(heads, s=2)
            nc.vector.tensor_tensor(g_v, bank[6][:, 0:P].rearrange("p (c h) -> p h c", h=16)[:, 8:16, :],
                                    small[:, 8:16].unsqueeze(2).to_broadcast([P, HEADS, TILES]), ALU.add
                                    ).then_inc(g_step, 1)
            dve.wait_ge(g_step, 1)
            stt(out=e_kd[:, :, :], in0=g_tab[:, :, :], scalar=-1.0, in1=g_tab[:, :, :], op0=ALU.mult, op1=ALU.max
                ).then_inc(g_step, 1)
            dve.wait_ge(g_exp, 3)
            stt(out=g_tab[:, :, :], in0=g_tab[:, :, :], scalar=0.0, in1=e_gl[:, :, :], op0=ALU.max, op1=ALU.add
                ).then_inc(g_step, 1)
            dve.wait_ge(g_step, 3)
            stt(out=g_v, in0=g_v, scalar=-1.0, in1=small[:, 16:24].unsqueeze(2).to_broadcast([P, HEADS, TILES]),
                op0=ALU.mult, op1=ALU.mult).then_inc(g_step, 1)
            for k in range(KT):
                sum_ada(k, 2 * D_MODEL, 3 * D_MODEL, KT)
            convolve(0, 2)
            dve.wait_ge(gate_mm, 1)
            for n in range(2):
                gb = gate_bc[:, n * 512:(n + 1) * 512]
                nc.vector.tensor_tensor(gb, bank[2 + n][:, :], gb, ALU.add).then_inc(gate_done, 1)
            convolve(0, 3)
            with dve.Fori(0, UNITS - 1) as u:
                phase_b(u)
                phase_a(u + 1, u)
            phase_b(UNITS - 1, last=True)
            phase_a(None, UNITS - 1)
            dve.wait_ge(fw_in, 16)
            for t in range(TILES):
                dve.wait_ge(fin_pow, t + 1)
                if t >= 2:
                    dve.wait_ge(stored[t % 2], 16 * (t // 2))
                stt(out=fin[:, t % 2, :], in0=y[:, t, :], scalar=frs[:, t:t + 1], in1=w_raw[:, 0, :],
                    op0=ALU.mult, op1=ALU.mult).then_inc(fin_done, 1)

        @block.gpsimd
        def _(pool):
            prime(pool, "gpsimd")
            step = [0]

            def then(i):
                step[0] += 1
                i.then_inc(const_step, 1)
                pool.wait_ge(const_step, step[0])

            def select(ap, pattern, base, channel, op, fill):
                then(nc.gpsimd.affine_select(out=ap, in_=ap, compare_op=op, fill=fill, base=base, pattern=pattern,
                                             channel_multiplier=channel))

            for ap, v in ((ones[:, :], 1.0), (ident[:, :], 0.0), (upto[:, :], 1.0), (after[:, :], 1.0),
                          (lower[:, :], 1.0), (pair_mask[:, :, :], 0.0), (neg_half[:, :], -0.5), (l2_eps4[:, :], 4 * L2_EPS),
                          (even[:, :], 0.0), (odd[:, :], 0.0)):
                nc.gpsimd.memset(ap, v)
            then(nc.gpsimd.memset(blk_id[:, :, :], 0.0))
            select(ident[:, :], [[-1, P]], 0, 1, ALU.not_equal, 1.0)
            nc.gpsimd.sem_inc(consts, 1)
            select(upto[:, :], [[1, P]], 0, -1, ALU.is_ge, 0.0)
            select(after[:, :], [[-1, P]], -1, 1, ALU.is_ge, 0.0)
            select(lower[:, :], [[-1, P]], 0, 1, ALU.is_ge, 0.0)
            select(blk_id[:, :, :], [[1, BLK], [-1, BLK]], 0, 0, ALU.not_equal, 1.0)
            for lv in range(3):
                s = BLK << lv
                n = P // (2 * s)
                m = pair_mask[:, lv, :].rearrange("p (b q w) -> p b q w", q=2, w=s)[:, :, 1, :]
                then(nc.gpsimd.memset(m, 1.0))
                select(m, [[-2 * s, n], [0, s]], 0, 1, ALU.is_ge, 0.0)
                select(m, [[2 * s, n], [0, s]], s - 1, -1, ALU.is_ge, 0.0)
            nc.gpsimd.memset(even[:, 0:UNITS:2], 1.0)
            nc.gpsimd.memset(odd[:, 1:UNITS:2], 1.0)
            nc.gpsimd.memset(t16[:, :, :], 0.0)
            nc.gpsimd.memset(u16[:, :, :], 0.0)
            nc.gpsimd.memset(state[:, :], 0.0)
            nc.gpsimd.memset(tails[:, :, :], 0.0)
            then(nc.gpsimd.memset(pre[:, :, 0:4], 0.0))
            nc.gpsimd.sem_inc(consts, 1)

            def row_power(half):
                xs_ = xss[:, 4 * half:4 * half + 4]
                pool.wait_ge(x_squared, 4 * half + 4)
                nc.gpsimd.tensor_scalar(xs_, xs_, 1.0 / D_MODEL, NORM_EPS, ALU.mult, ALU.add).then_inc(x_mean, 1)
                pool.wait_ge(x_mean, half + 1)
                nc.gpsimd.tensor_tensor(xrs[:, 4 * half:4 * half + 4], xs_, neg_half[:, 0:4], ALU.pow
                                        ).then_inc(x_pow, 1)

            def split_lo(u, k):
                passed(pool, "w_hi_done", u, k + 1)
                if k < PIECES:
                    dst, hi, src = w_lo[:, k % 2, :, :], w_hi[:, k % 2, :, :], w_raw_k[:, k % 2, :, :]
                else:
                    dst, hi, src = wo_lo[:, k - PIECES, :], wo_hi[:, k - PIECES, :], w_raw[:, k % 2, :]
                nc.gpsimd.tensor_tensor(dst, src, hi.bitcast(F32), ALU.subtract).then_inc(S["w_lo_done"], 1)

            def mask_g(u):
                passed(pool, "decay_mm", u, 0)
                nc.gpsimd.tensor_tensor(g_after, after[:, :].unsqueeze(1).to_broadcast([P, NCH, P]),
                                        g_tab[:, u, :].unsqueeze(2).to_broadcast([P, NCH, P]), ALU.mult
                                        ).then_inc(S["g_after_done"], 1)

            def og_low(g, c):
                passed(pool, "og_hi_done", g, c + 1)
                nc.gpsimd.tensor_tensor(og_lo[:, :, :], og, og_hi[:, :, :].bitcast(F32), ALU.subtract
                                        ).then_inc(S["og_lo_done"], 1)

            def phase_a(u, g):
                for c in range(NCH):
                    if u is not None:
                        split_lo(u, c + 1)
                    if c > 0:
                        og_low(g, c - 1)
                    passed(pool, "o_mean", g, c + 1)
                    nc.gpsimd.tensor_tensor(oss[:, 2:3], oss[:, 1:2], neg_half[:, 0:1], ALU.pow
                                            ).then_inc(S["o_pow"], 1)
                og_low(g, 3)
                if u is not None:
                    mask_g(u)

            def phase_b(u, last=False):
                split_lo(u, 5)
                passed(pool, "squared", u, 8)
                nc.gpsimd.tensor_tensor(rs[:, :], st[:, :], l2_eps4[:, :], ALU.add).then_inc(S["norms_step"], 1)
                passed(pool, "norms_step", u, 1)
                nc.gpsimd.tensor_tensor(rs[:, :], rs[:, :], neg_half[:, :], ALU.pow).then_inc(S["norms_done"], 1)
                passed(pool, "decay_exp", u, 1)
                nc.gpsimd.tensor_tensor(decay, decay, lower[:, :].unsqueeze(1).to_broadcast([P, NCH, P]), ALU.mult
                                        ).then_inc(S["decay_done"], 1)
                split_lo(u, 6)
                split_lo(u, 7)
                passed(pool, "scalars_done", u, 1)
                for c in range(NCH):
                    passed(pool, "turned_out", u, c + 1)
                    nc.gpsimd.tensor_tensor(vt[:, c, :], vt[:, c, :], sc[:, 2, c:c + 1].to_broadcast([P, DV]), ALU.mult
                                            ).then_inc(S["v_scaled"], 1)
                if not last:
                    split_lo(u + 1, 0)

            row_power(0)
            split_lo(0, 0)
            split_lo(0, 1)
            row_power(1)
            for k in (2, 3, 4):
                split_lo(0, k)
            pool.wait_ge(g_step, 4)
            mask_g(0)
            with pool.Fori(0, UNITS - 1) as u:
                phase_b(u)
                phase_a(u + 1, u)
            phase_b(UNITS - 1, last=True)
            phase_a(None, UNITS - 1)
            for t in range(TILES):
                pool.wait_ge(fin_squared, t + 1)
                nc.gpsimd.tensor_scalar(fss[:, t:t + 1], fss[:, t:t + 1], 1.0 / D_MODEL, NORM_EPS, ALU.mult, ALU.add
                                        ).then_inc(fin_step, 1)
                pool.wait_ge(fin_step, t + 1)
                nc.gpsimd.tensor_tensor(frs[:, t:t + 1], fss[:, t:t + 1], neg_half[:, 0:1], ALU.pow
                                        ).then_inc(fin_pow, 1)

_INS = ["x", "c", "ada_w", "ada_b", "norm_w", "gdn_w_in", "gdn_conv_w", "gdn_a_log", "gdn_dt_bias",
        "gdn_norm_w", "gdn_w_out", "final_norm_w"]


def kernel(**inputs):
    import numpy as np
    import concourse.bacc as bacc
    from concourse.bass_utils import run_bass_kernel_spmd

    nc = bacc.Bacc("TRN2", target_bir_lowering=False, num_devices=1)
    arrays, args = {}, []
    for name in _INS:
        a = np.ascontiguousarray(inputs[name])
        arrays[f"in_{name}"] = a
        args.append(nc.dram_tensor(f"in_{name}", a.shape, mybir.dt.from_np(a.dtype), kind="ExternalInput").ap())
    args.append(nc.dram_tensor("out_0", (1, SEQ, D_MODEL), F32, kind="ExternalOutput").ap())
    build(nc, *args)
    r = run_bass_kernel_spmd(nc, [arrays], core_ids=[0])
    return r.results[0]["out_0"]
```

```python
from contextlib import ExitStack

import concourse.bass as bass
from concourse import mybir

F32 = mybir.dt.float32
F32R = mybir.dt.float32r
ALU = mybir.AluOpType
ACT = mybir.ActivationFunctionType

P = 128
D_MODEL = 1024
SEQ = 1024
HEADS = 8
DK = 128
DV = 256
NORM_EPS = 1e-6
L2_EPS = 1e-6

KT = D_MODEL // P
UNITS = 2 * HEADS
HALF = SEQ // 2
NCH = HALF // P
TILES = SEQ // P
TAPS = 4
PIECES = 6
CONVED = 4
WTILES = 8
MM = 3 * KT
Z_OFF = 2 * HEADS * DK + HEADS * DV
V_OFF = 2 * HEADS * DK
BA_OFF = Z_OFF + HEADS * DV
BLK = 16
NBLK = P // BLK


def build(nc, x, c, ada_w, ada_b, norm_w, w_in, conv_w, a_log, dt_bias, gdn_norm_w, w_out,
          final_norm_w, out):
    ctx = ExitStack()
    with ctx:
        def sb(name, shape, dt=F32):
            return ctx.enter_context(nc.sbuf_tensor(name, shape, dt))

        def sem(name):
            return ctx.enter_context(nc.semaphore(name))

        h_hi = sb("h_hi", [P, KT, SEQ], F32R)
        h_lo = sb("h_lo", [P, KT, SEQ], F32R)
        y = sb("y", [P, TILES, D_MODEL])
        w_raw = sb("w_raw", [P, 2, 1024])
        w_hi = sb("w_hi", [P, 2, KT, P], F32R)
        w_lo = sb("w_lo", [P, 2, KT, P], F32R)
        wo_hi = sb("wo_hi", [P, 2, D_MODEL], F32R)
        wo_lo = sb("wo_lo", [P, 2, D_MODEL], F32R)
        og_hi = sb("og_hi", [P, 2, P], F32R)
        og_lo = sb("og_lo", [P, 2, P], F32R)
        gate_bc = sb("gate_bc", [P, D_MODEL])
        pre = sb("pre", [P, 2, HALF + 4])
        work = sb("work", [P, 12288])
        pm = sb("pm", [P, 2, NCH, P])
        ident = sb("ident", [P, P])
        upto = sb("upto", [P, P])
        after = sb("after", [P, P])
        lower = sb("lower", [P, P])
        pair_mask = sb("pair_mask", [P, 3, P])
        diag_mask = sb("diag_mask", [P, P])
        ones = sb("ones", [P, P])
        fss = sb("fss", [P, TILES])
        frs = sb("frs", [P, TILES])
        cw = sb("cw", [P, TAPS * 32])
        rows_t = sb("rows_t", [P, 34])
        mod = sb("mod", [P, 24])
        g_tab = sb("g_tab", [P, UNITS, NCH])
        beta = sb("beta", [P, UNITS, NCH])
        e_gc = sb("e_gc", [P, UNITS, NCH])
        e_kd = sb("e_kd", [P, UNITS, NCH])
        e_gl = sb("e_gl", [P, UNITS, NCH])
        even = sb("even", [P, UNITS])
        odd = sb("odd", [P, UNITS])
        tails = sb("tails", [P, CONVED, 4])
        st = sb("st", [P, 2 * NCH])
        rs = sb("rs", [P, 2 * NCH])
        sc = sb("sc", [P, 6, NCH])
        sn = sb("sn", [P, 2, NCH])
        oss = sb("oss", [P, 4])
        neg_half = sb("neg_half", [P, 8])
        l2_eps4 = sb("l2_eps4", [P, 2 * NCH])
        small = sb("small", [P, 64])
        blk_id = sb("blk_id", [NBLK * NCH, BLK, BLK])
        state = sb("state", [P, DV])

        def part(at, n, **dims):
            v = work[:, at:at + n]
            return v.rearrange(dims.pop("to"), **dims) if dims else v

        cv = part(0, 2048, to="p (m t) -> p m t", m=4)
        th = part(2048, 1024, to="p (m t) -> p m t", m=2)
        kq = part(4096, 1024, to="p (m t) -> p m t", m=2)
        vt = part(5120, 1024, to="p (c t) -> p c t", c=NCH)
        kdec = part(6144, 512, to="p (c t) -> p c t", c=NCH)
        attn_t = part(6656, 512, to="p (c t) -> p c t", c=NCH)
        u_fin = part(7168, 512, to="p (c t) -> p c t", c=NCH)
        zt = part(7680, 1024, to="p (m t) -> p m t", m=2)
        nmat = part(8704, 512, to="p (c t) -> p c t", c=NCH)
        decay = part(9216, 512, to="p (c t) -> p c t", c=NCH)
        g_after = part(9728, 512, to="p (c t) -> p c t", c=NCH)
        attn = part(10240, 512, to="p (c t) -> p c t", c=NCH)
        pm_last = part(10752, 256, to="p (c t) -> p c t", c=NCH)
        tm = part(11264, 512, to="p (c t) -> p c t", c=NCH)
        blk_n, blk_y, blk_tmp = (work[0:NBLK * NCH, o:o + BLK * BLK].rearrange("p (i j) -> p i j", i=BLK)
                                 for o in (9728, 9984, 3072))
        r_rhs = part(10240, 256)
        xs = part(10496, 256)
        qss = part(10752, 256)
        o_raw = part(11008, 256)
        o_n = part(11264, 256)
        og = part(11520, 256, to="p (m t) -> p m t", m=2)
        junk = part(11776, 256)
        t_comp = part(3328, NCH * BLK, to="p (c t) -> p c t", c=NCH)
        junk_b = part(3392, P)
        ada_buf = part(0, 4096, to="p (s n) -> p s n", s=2)
        ada_acc = part(4096, 3072)
        gate_buf = part(4096, 2048, to="p (s n) -> p s n", s=2)
        xn = part(7168, 4096, to="p (c d) -> p c d", c=4)
        hf = part(11264, 1024, to="p (s t) -> p s t", s=2)
        rows = w_raw[:, 1, 0:2 * P].rearrange("p (r t) -> p r t", r=2)
        ba_rows = part(1024, SEQ)[0:16, :]
        c_col = sb("c_col", [P, KT])
        c_th = sb("c_th", [P, KT])
        xss = sb("xss", [P, TILES])
        xrs = sb("xrs", [P, TILES])
        wba_raw = junk_b.rearrange("p (k n) -> p k n", k=KT)
        wba_hi = wo_hi[:, 0, 0:KT * 16].rearrange("p (k n) -> p k n", k=KT)
        wba_lo = wo_lo[:, 0, 0:KT * 16].rearrange("p (k n) -> p k n", k=KT)

        bank = [ctx.enter_context(nc.psum_tensor(f"bank{i}", [P, 512], F32)) for i in range(8)]

        PER = dict(
            w_hi_done=6, w_lo_done=6, wo_gated=2, wo_hi_done=2, wo_lo_done=2,
            projected=6, evacuated=6, conv_done=4, tanh_done=6, silu_done=6,
            conv_step=16,
            g_after_done=1, decay_mm=1, decay_exp=1, decay_done=1,
            k_turned=2, kk_done=1, k_squared=4, k_norm_step=1, k_norm=1, k_scalar=2, n_done=1, kdec_done=1,
            q_turned=1, qk_done=1, q_squared=4, q_norm_step=1, q_norm=1, scalar_step=1, scalars_done=1,
            kq_done=1, attn_done=1, attn_turned=1, attn_out=1, v_turned=1, v_scaled=4,
            base_step=31, t_done=1, t_turned=1, u_out=1,
            merge_p=3, merge_p_out=3, merge_d=3, merge_d_out=3,
            ks_done=4, qs_done=4, r_done=4, qs_scaled=4, x_done=4, x_out=4,
            kv_done=4, av_done=4, state_done=5, o_done=4, o_squared=4, o_mean=4, o_pow=4,
            o_scaled=4, o_turned=4, og_done=4, og_hi_done=4, og_lo_done=4,
            out_done=4, y_added=4,
        )
        S = {name: sem(name) for name in PER}
        MAKERS = dict(
            tensor="projected decay_mm k_turned kk_done q_turned qk_done attn_turned v_turned t_turned merge_p "
                   "merge_d ks_done qs_done x_done kv_done av_done o_turned out_done",
            scalar="w_hi_done wo_hi_done evacuated tanh_done decay_exp k_squared q_squared attn_out v_scaled "
                   "u_out qs_scaled x_out o_squared og_hi_done",
            vector="conv_done silu_done conv_step k_scalar n_done kdec_done scalar_step scalars_done kq_done "
                   "attn_done base_step t_done merge_p_out merge_d_out r_done state_done o_done o_mean "
                   "o_scaled og_done y_added",
            gpsimd="w_lo_done wo_gated wo_lo_done g_after_done decay_done k_norm_step k_norm q_norm_step q_norm "
                   "o_pow og_lo_done",
        )
        raw_in = [sem(f"raw_in{i}") for i in range(2)]
        blk_in = sem("blk_in")
        n_stored = sem("n_stored")
        t_stored = sem("t_stored")
        t_back = sem("t_back")
        x_in = [sem(f"x_in{i}") for i in range(2)]
        ada_in = [sem(f"ada_in{i}") for i in range(2)]
        rows_in = sem("rows_in")
        c_in = sem("c_in")
        wba_in = sem("wba_in")
        bias_in = sem("bias_in")
        fw_in = sem("fw_in")
        stored = [sem(f"stored{i}") for i in range(2)]
        const_step = sem("const_step")
        consts = sem("consts")
        rows_turned, rows_out = sem("rows_turned"), sem("rows_out")
        c_step, x_squared, x_mean, x_pow = sem("c_step"), sem("x_squared"), sem("x_mean"), sem("x_pow")
        xn_done, x_turned, h_done, h_split = sem("xn_done"), sem("x_turned"), sem("h_done"), sem("h_split")
        hi_step = sem("hi_step")
        ada_summed, mod_mm, mod_done = sem("ada_summed"), sem("mod_mm"), sem("mod_done")
        wba_split, ba_mm, ba_out, ba_turned, g_step, g_exp = sem("wba_split"), sem("ba_mm"), sem("ba_out"), sem("ba_turned"), sem("g_step"), sem("g_exp")
        beta_step = sem("beta_step")
        sums_mm, tables_done, gate_mm, gate_done = (sem("sums_mm"), sem("tables_done"), sem("gate_mm"),
                                                     sem("gate_done"))
        fin_squared, fin_pow, fin_done, fin_step = (sem("fin_squared"), sem("fin_pow"), sem("fin_done"),
                                                    sem("fin_step"))

        def at(name, u, n):
            return PER[name] * (u + 1) + n

        def prime(eng, which):
            for name in MAKERS[which].split():
                eng.sem_inc(S[name], PER[name])

        def passed(eng, name, u, n):
            eng.wait_ge(S[name], at(name, u, n))

        def tile_landed(eng, u, k):
            eng.wait_ge(raw_in[k % 2], 16 * (4 * u + k // 2 + 1))

        x_v = x.rearrange("b (t p) d -> p (b t) d", p=P)
        out_v = out.rearrange("b (t p) d -> p (b t) d", p=P)
        ada_v = ada_w.rearrange("o (p k) n -> p (o k) n", k=KT)
        w_in_v = w_in.rearrange("o (k p) n -> p (o k) n", p=P)
        w_out_v = w_out.rearrange("o (h k p) n -> p (o h) k n", k=2, p=P)
        w_raw_k = w_raw[:, :, :].rearrange("p s (k n) -> p s k n", k=KT)
        h_hi_v = h_hi[:, :, :].rearrange("p k (s t) -> p k s t", s=2)
        h_lo_v = h_lo[:, :, :].rearrange("p k (s t) -> p k s t", s=2)

        y_v = y[:, :, :].rearrange("p (s c) d -> p s c d", s=2)

        blk_gap = BLK * (P + 1)
        n_dram = nc.dram_tensor("n_dram", (NCH * NBLK * blk_gap,), F32).ap()
        n_rows = bass.AP(n_dram.tensor, 0, [[P, P], [NBLK * blk_gap, NCH], [1, P]])
        n_blocks = bass.AP(n_dram.tensor, 0, [[blk_gap, NBLK * NCH], [P, BLK], [1, BLK]])
        t_dram = nc.dram_tensor("t_dram", (NBLK * NCH, BLK, BLK), F32).ap()
        t_rows = bass.AP(t_dram.tensor, 0, [[BLK, P], [P * BLK, NCH], [1, BLK]])

        def pairs(m, lv):
            return m.rearrange("p c (b q w) -> p c b q w", q=2, w=BLK << lv)

        def halves(b, lv, at=0):
            return b[:, at:at + NCH * 64].rearrange("p (c b w) -> p c b w", c=NCH, w=BLK << lv)

        FILL_A = ((6, 6, 4), (6, 6, 4), (0, 4, 4), (2, 2, 4))
        FILL_TAIL = (12, 10)
        START_A = 20
        START_B = START_A + sum(sum(f) for f in FILL_A) + sum(FILL_TAIL)
        FILL_MERGE = 5
        START_MERGE = PIECES * MM - 5 * FILL_MERGE
        START_T = START_MERGE - 4

        block = ctx.enter_context(nc.Block())

        @block.sync
        def _(sp):
            def load_tile(u, k, wait=None):
                slot = k % 2
                if wait is not None:
                    wait()
                head = u // 2
                if k < PIECES:
                    off = ((HEADS + head) * DK, head * DK, V_OFF + head * DV, V_OFF + P + head * DV,
                           Z_OFF + head * DV, Z_OFF + P + head * DV)[k]
                    src, dst = w_in_v[:, :, bass.ds(off, P)], w_raw_k[:, slot, :, :]
                else:
                    src, dst = w_out_v[:, head, k - PIECES, :], w_raw[:, slot, :]
                sp.dma_start(dst, src).then_inc(raw_in[slot], 16)

            def next_tile(u, k):
                if k < 2:
                    load_tile(u, k, lambda: sp.wait_ge(S["wo_lo_done"], 2 * u + k + 1))
                else:
                    load_tile(u, k, lambda: passed(sp, "w_lo_done", u, k - 1))

            def invert_out(u):
                passed(sp, "n_done", u, 1)
                sp.dma_start(n_rows, nmat).then_inc(n_stored, 16)
                sp.wait_ge(n_stored, 16 * (u + 1))
                passed(sp, "decay_mm", u, 1)
                sp.dma_start(blk_n[:, :, :], n_blocks).then_inc(blk_in, 16)

            def invert_back(u):
                passed(sp, "base_step", u, 2 * BLK - 1)
                sp.dma_start(t_dram, blk_y[:, :, :]).then_inc(t_stored, 16)
                sp.wait_ge(t_stored, 16 * (u + 1))
                sp.dma_start(t_comp, t_rows).then_inc(t_back, 16)

            sp.dma_start(rows[:, 0, :], conv_w.rearrange("o j (t p) -> (o j t) p", p=P)).then_inc(rows_in, 16)
            sp.dma_start(rows[0:24, 1, :], ada_b.rearrange("o (t p) -> (o t) p", p=P)).then_inc(rows_in, 16)
            sp.dma_start(rows[24:32, 1, :], norm_w.rearrange("o (t p) -> (o t) p", p=P)).then_inc(rows_in, 16)
            sp.dma_start(rows[32:34, 1, :], gdn_norm_w.rearrange("o (t p) -> (o t) p", p=P)).then_inc(rows_in, 16)
            sp.dma_start(c_col[:, :], c.rearrange("o (p k) -> p (o k)", k=KT)).then_inc(c_in, 16)
            sp.dma_start(y[:, 0:4, :], x_v[:, 0:4, :]).then_inc(x_in[0], 16)
            load_tile(0, 0)
            for k in range(KT):
                if k == 4:
                    sp.wait_ge(rows_turned, 1)
                    load_tile(0, 1)
                if k >= 2:
                    sp.wait_ge(ada_summed, k - 1)
                sp.dma_start(ada_buf[:, k % 2, :], ada_v[:, k, 0:2 * D_MODEL]).then_inc(ada_in[k % 2], 16)
            sp.wait_ge(consts, 2)
            sp.dma_start(y[:, 4:8, :], x_v[:, 4:8, :]).then_inc(x_in[1], 16)
            sp.wait_ge(ada_summed, KT)
            sp.dma_start(wba_raw, w_in_v[:, :, BA_OFF:BA_OFF + 16]).then_inc(wba_in, 16)
            sp.dma_start(small[:, 0:8], a_log.partition_broadcast(P)).then_inc(bias_in, 16)
            sp.dma_start(small[:, 8:16], dt_bias.partition_broadcast(P)).then_inc(bias_in, 16)
            sp.dma_start(gate_bc[:, :], ada_b[0:1, 2 * D_MODEL:].partition_broadcast(P)).then_inc(bias_in, 16)
            next_tile(0, 2)
            next_tile(0, 3)
            for k in range(KT):
                if k == 0:
                    sp.wait_ge(mod_mm, 1)
                if k >= 2:
                    sp.wait_ge(ada_summed, KT + k - 1)
                sp.dma_start(gate_buf[:, k % 2, :], ada_v[:, k, 2 * D_MODEL:]).then_inc(ada_in[k % 2], 16)
                if k == 5:
                    next_tile(0, 4)
            invert_out(0)
            next_tile(0, 5)

            def phase_b(u, last=False):
                next_tile(u, 6)
                invert_back(u)
                next_tile(u, 7)
                if not last:
                    for k in range(4):
                        next_tile(u + 1, k)

            with sp.Fori(0, UNITS - 1) as u:
                phase_b(u)
                next_tile(u + 1, 4)
                next_tile(u + 1, 5)
                invert_out(u + 1)
            phase_b(UNITS - 1, last=True)

            passed(sp, "wo_lo_done", UNITS - 1, 2)
            sp.dma_start(w_raw[:, 0, :], final_norm_w.rearrange("(o n) -> o n", o=1).partition_broadcast(P)
                         ).then_inc(fw_in, 16)
            for t in range(TILES):
                sp.wait_ge(fin_done, t + 1)
                sp.dma_start(out_v[:, t, :], y[:, t, :]).then_inc(stored[t % 2], 16)
            for i in range(2):
                sp.wait_ge(stored[i], 16 * TILES // 2)

        @block.tensor
        def _(pe):
            prime(pe, "tensor")

            def project(u, first, last):
                for n in range(first, last):
                    m, r = divmod(n, MM)
                    k, part_no = divmod(r, 3)
                    if r == 0:
                        passed(pe, "w_lo_done", u, m + 1)
                        passed(pe, "evacuated", u, m - 1)
                    w, h = ((w_hi, h_hi_v), (w_hi, h_lo_v), (w_lo, h_hi_v))[part_no]
                    mm = nc.tensor.matmul(bank[m % 2][:, :], w[:, m % 2, k, :], h[:, k, u % 2, :],
                                          start=(r == 0), stop=(r == MM - 1))
                    if r == MM - 1:
                        mm.then_inc(S["projected"], 1)

            def turn_o(g, c):
                passed(pe, "o_scaled", g, c + 1)
                passed(pe, "qs_scaled", g, min(c + 2, 4))
                for m in range(2):
                    mm = nc.tensor.transpose(bank[3][:, m * P:(m + 1) * P], o_n[:, m * P:(m + 1) * P], ident[:, :])
                mm.then_inc(S["o_turned"], 1)

            def out_project(g, c, u, n):
                if c == 0 and n == 0:
                    passed(pe, "wo_lo_done", g, 2)
                    if u is not None:
                        passed(pe, "decay_exp", u, 1)
                if n == 0:
                    passed(pe, "og_lo_done", g, c + 1)
                    passed(pe, "y_added", g, c)
                for m in range(2):
                    for q, (a, w) in enumerate(((og_hi, wo_hi), (og_hi, wo_lo), (og_lo, wo_hi))):
                        mm = nc.tensor.matmul(bank[6 + n][:, :], a[:, m, :], w[:, m, n * 512:(n + 1) * 512],
                                              start=(m == 0 and q == 0), stop=(m == 1 and q == 2))
                if n == 1:
                    mm.then_inc(S["out_done"], 1)

            def decay_exponents(u):
                passed(pe, "g_after_done", u, 1)
                passed(pe, "attn_out", u, 0)
                nc.tensor.matmul(bank[7][:, :], upto[:, :], g_after.rearrange("p c t -> p (c t)"),
                                 start=True, stop=True).then_inc(S["decay_mm"], 1)

            def turn_k(u, which):
                passed(pe, "silu_done", u, 1)
                passed(pe, "merge_d_out" if which == 0 else "n_done", u, which)
                for c in range(NCH):
                    mm = nc.tensor.transpose(bank[5][:, c * P:(c + 1) * P], cv[:, 0, c * P:(c + 1) * P], ident[:, :])
                mm.then_inc(S["k_turned"], 1)

            def k_gram(u):
                passed(pe, "k_squared", u, 4)
                for c in range(NCH):
                    k_c = cv[:, 0, c * P:(c + 1) * P]
                    mm = nc.tensor.matmul(bank[5][:, c * P:(c + 1) * P], k_c, k_c, start=True, stop=True)
                mm.then_inc(S["kk_done"], 1)

            def phase_a(u, g):
                pos = [START_A]

                def fill(n):
                    if u is not None:
                        project(u, pos[0], pos[0] + n)
                        pos[0] += n

                for c in range(NCH):
                    passed(pe, "state_done", g, c + 1)
                    if c == 0:
                        passed(pe, "kq_done", g, 1)
                        passed(pe, "v_scaled", g, 4)
                    passed(pe, "o_done", g, c)
                    nc.tensor.matmul(bank[2][:, 0:DV], kq[:, 0, c * P:(c + 1) * P], state[:, :],
                                     start=True, stop=True).then_inc(S["ks_done"], 1)
                    passed(pe, "og_done", g, max(c - 1, 0))
                    nc.tensor.matmul(bank[3][:, 0:DV], kq[:, 1, c * P:(c + 1) * P], state[:, :],
                                     start=True, stop=True).then_inc(S["qs_done"], 1)
                    if c >= 2:
                        out_project(g, c - 2, u, 0)
                    fill(FILL_A[c][0])
                    if c == 0:
                        passed(pe, "merge_d_out", g, 3)
                    else:
                        passed(pe, "x_out", g, c)
                    passed(pe, "r_done", g, c + 1)
                    nc.tensor.matmul(bank[4][:, 0:DV], u_fin[:, c, :], r_rhs, start=True, stop=True
                                     ).then_inc(S["x_done"], 1)
                    if c == 2 and u is not None:
                        turn_k(u, 0)
                    if c >= 2:
                        out_project(g, c - 2, u, 1)
                    fill(FILL_A[c][1])
                    if c == 0 and u is not None:
                        decay_exponents(u)
                    if c > 0:
                        turn_o(g, c - 1)
                    passed(pe, "x_out", g, c + 1)
                    nc.tensor.matmul(bank[4][:, DV:2 * DV], kdec[:, c, :], xs, start=True, stop=True
                                     ).then_inc(S["kv_done"], 1)
                    if c == 0:
                        passed(pe, "attn_out", g, 1)
                    nc.tensor.matmul(bank[2][:, 0:DV], attn_t[:, c, :], xs, start=True, stop=True
                                     ).then_inc(S["av_done"], 1)
                    fill(FILL_A[c][2])
                    if c == 2 and u is not None:
                        k_gram(u)
                fill(FILL_TAIL[0])
                turn_o(g, NCH - 1)
                for n in range(2):
                    out_project(g, NCH - 2, u, n)
                fill(FILL_TAIL[1])
                for n in range(2):
                    out_project(g, NCH - 1, u, n)

            def phase_b(u, last=False):
                project(u, START_B, START_B + 6)
                passed(pe, "silu_done", u, 2)
                passed(pe, "x_out", u, 0)
                passed(pe, "state_done", u, 0)
                for c in range(NCH):
                    mm = nc.tensor.transpose(bank[4][:, c * P:(c + 1) * P], cv[:, 1, c * P:(c + 1) * P], ident[:, :])
                mm.then_inc(S["q_turned"], 1)
                turn_k(u, 1)
                passed(pe, "o_done", u, 0)
                for c in range(NCH):
                    mm = nc.tensor.matmul(bank[2][:, c * P:(c + 1) * P], cv[:, 1, c * P:(c + 1) * P],
                                          cv[:, 0, c * P:(c + 1) * P], start=True, stop=True)
                mm.then_inc(S["qk_done"], 1)
                project(u, START_B + 6, START_T)
                passed(pe, "t_done", u, 1)
                passed(pe, "q_squared", u, 4)
                for c in range(NCH):
                    mm = nc.tensor.transpose(bank[4][:, c * P:(c + 1) * P], tm[:, c, :], ident[:, :])
                mm.then_inc(S["t_turned"], 1)
                project(u, START_T, START_MERGE)
                passed(pe, "u_out", u, 1)
                passed(pe, "kdec_done", u, 1)
                passed(pe, "y_added", u, 0)
                pos = START_MERGE
                for lv in range(3):
                    d_bank = bank[(6, 4, 6)[lv]]
                    if lv > 0:
                        passed(pe, "merge_d_out", u, lv)
                    p_bank = halves(bank[5], lv, (lv % 2) * DV)
                    for c in range(NCH):
                        mm = nc.tensor.matmul(p_bank[:, c, :, :], nmat[:, c, :], pairs(u_fin, lv)[:, c, :, 1, :],
                                              start=True, stop=True)
                    mm.then_inc(S["merge_p"], 1)
                    project(u, pos, pos + FILL_MERGE)
                    pos += FILL_MERGE
                    passed(pe, "merge_p_out", u, lv + 1)
                    if lv < 2:
                        for c in range(NCH):
                            nc.tensor.matmul(halves(d_bank, lv)[:, c, :, :], pm[:, lv, c, :],
                                             pairs(tm, lv)[:, c, :, 0, :], start=True, stop=True)
                    for c in range(NCH):
                        p_c = pairs(pm[:, lv, :, :], lv)[:, c, :, 1, :] if lv < 2 else pm_last[:, c, :]
                        out_c = halves(d_bank, lv, DV)[:, c, :, :] if lv < 2 else d_bank[:, DV + c * 64:DV + (c + 1) * 64]
                        mm = nc.tensor.matmul(out_c, tm[:, c, :], p_c, start=True, stop=True)
                    mm.then_inc(S["merge_d"], 1)
                    if lv < 2:
                        project(u, pos, pos + FILL_MERGE)
                        pos += FILL_MERGE
                passed(pe, "attn_done", u, 1)
                for c in range(NCH):
                    mm = nc.tensor.transpose(bank[7][:, c * P:(c + 1) * P], attn[:, c, :], ident[:, :])
                mm.then_inc(S["attn_turned"], 1)
                if not last:
                    project(u + 1, 0, START_A - 8)
                passed(pe, "silu_done", u, 4)
                passed(pe, "og_done", u, 0)
                for c in range(NCH):
                    for m in range(2):
                        o = (c % 2) * DV + m * P
                        mm = nc.tensor.transpose(bank[2 + c // 2][:, o:o + P], cv[:, 2 + m, c * P:(c + 1) * P],
                                                 ident[:, :])
                mm.then_inc(S["v_turned"], 1)
                if not last:
                    project(u + 1, START_A - 8, START_A)

            pe.wait_ge(rows_in, 64)
            pe.wait_ge(consts, 1)
            nc.tensor.transpose(bank[7][:, 0:P], rows[:, 0, :], ident[:, :])
            nc.tensor.transpose(bank[7][:, P:P + 34], rows[0:34, 1, :], ident[0:34, 0:34]).then_inc(rows_turned, 1)

            def turn_x(half, first, last):
                for k in range(first, last):
                    if half == 1 or k >= 4:
                        pe.wait_ge(h_done, 8 * half + k - 3)
                    for t in range(4):
                        mm = nc.tensor.transpose(bank[2 + k % 4][:, t * P:(t + 1) * P],
                                                 xn[:, t, k * P:(k + 1) * P], ident[:, :])
                    mm.then_inc(x_turned, 1)

            pe.wait_ge(xn_done, 4)
            turn_x(0, 0, 4)
            pe.wait_ge(ada_summed, KT)
            for j in range(16):
                mm = nc.tensor.matmul(bank[6][:, j:j + 1], ada_acc[:, j * P:(j + 1) * P], ones[:, 0:1],
                                      start=True, stop=True)
            mm.then_inc(mod_mm, 1)
            turn_x(0, 4, KT)
            pe.wait_ge(h_split, KT)
            project(0, 0, 24)
            pe.wait_ge(xn_done, 8)
            turn_x(1, 0, KT)
            project(0, 24, 48)
            pe.wait_ge(wba_split, 2)
            pe.wait_ge(h_split, 2 * KT)
            pe.wait_ge(h_done, 2 * KT)
            for s in range(2):
                for k in range(KT):
                    for q, (h, w) in enumerate(((h_hi_v, wba_hi), (h_lo_v, wba_hi), (h_hi_v, wba_lo))):
                        mm = nc.tensor.matmul(bank[4 + s][0:16, :], w[:, k, :], h[:, k, s, :],
                                              start=(k == 0 and q == 0), stop=(k == KT - 1 and q == 2))
            mm.then_inc(ba_mm, 1)
            project(0, 48, 60)
            pe.wait_ge(ba_out, 1)
            pe.wait_ge(mod_done, 2)
            for t in range(TILES):
                mm = nc.tensor.transpose(bank[6][:, t * 16:(t + 1) * 16], ba_rows[:, t * P:(t + 1) * P],
                                         ident[0:16, 0:16])
            mm.then_inc(ba_turned, 1)
            project(0, 60, 72)
            pe.wait_ge(g_step, 4)
            gt = g_tab[:, :, :].rearrange("p u c -> p (u c)")
            for i, m in enumerate((upto, after, ones)):
                mm = nc.tensor.matmul(bank[4][:, i * 64:(i + 1) * 64], m[:, :], gt, start=True, stop=True)
            mm.then_inc(sums_mm, 1)
            pe.wait_ge(tables_done, 3)
            decay_exponents(0)
            turn_k(0, 0)
            k_gram(0)
            project(0, 72, START_B)
            pe.wait_ge(ada_summed, 2 * KT)
            pe.wait_ge(h_done, 2 * KT)
            for n in range(2):
                mm = nc.tensor.matmul(bank[2 + n][:, :], ones[:, :],
                                      ada_acc[:, 2 * D_MODEL + n * 512:2 * D_MODEL + (n + 1) * 512],
                                      start=True, stop=True)
            mm.then_inc(gate_mm, 1)
            pe.wait_ge(gate_done, 2)
            with pe.Fori(0, UNITS - 1) as u:
                phase_b(u)
                phase_a(u + 1, u)
            phase_b(UNITS - 1, last=True)
            phase_a(None, UNITS - 1)

        @block.scalar
        def _(act):
            prime(act, "scalar")

            def split_hi(u, k):
                if k < PIECES:
                    tile_landed(act, u, k)
                    passed(act, "projected", u, k - 1)
                    nc.scalar.activation(w_hi[:, k % 2, :, :], w_raw_k[:, k % 2, :, :], ACT.Copy
                                         ).then_inc(S["w_hi_done"], 1)
                else:
                    passed(act, "wo_gated", u, k - 5)
                    passed(act, "out_done", u, 0)
                    nc.scalar.activation(wo_hi[:, k - PIECES, :], w_raw[:, k % 2, :], ACT.Copy
                                         ).then_inc(S["wo_hi_done"], 1)

            def evacuate(u, m):
                passed(act, "projected", u, m + 1)
                if m < CONVED:
                    passed(act, "conv_done", u, m - 1)
                    nc.scalar.activation(pre[:, m % 2, 3:3 + HALF], bank[m % 2][:, :], ACT.Copy
                                         ).then_inc(S["evacuated"], 1)
                else:
                    passed(act, "silu_done", u, m - 1)
                    nc.scalar.activation(th[:, m % 2, :], bank[m % 2][:, :], ACT.Tanh, scale=0.5
                                         ).then_inc(S["tanh_done"], 1)
                    passed(act, "og_done", u, 0)
                    nc.scalar.activation(zt[:, m - 4, :], bank[m % 2][:, :], ACT.Copy
                                         ).then_inc(S["evacuated"], 1)

            def tanh(u, m):
                passed(act, "conv_done", u, m + 1)
                passed(act, "silu_done", u, m - 1)
                nc.scalar.activation(th[:, m % 2, :], cv[:, m, :], ACT.Tanh, scale=0.5
                                     ).then_inc(S["tanh_done"], 1)

            def og_high(g, c):
                passed(act, "og_done", g, c + 1)
                passed(act, "out_done", g, c)
                nc.scalar.activation(og_hi[:, :, :], og, ACT.Copy).then_inc(S["og_hi_done"], 1)

            def square_k(u):
                passed(act, "k_turned", u, 1)
                passed(act, "k_norm", u, 0)
                for c in range(NCH):
                    if c == 0:
                        passed(act, "q_squared", u, 0)
                    passed(act, "k_squared", u, c)
                    nc.scalar.activation(junk_b, bank[5][:, c * P:(c + 1) * P], ACT.Square,
                                         accum_out=st[:, c:c + 1]).then_inc(S["k_squared"], 1)

            def decay_exp(u):
                passed(act, "decay_mm", u, 1)
                passed(act, "attn_done", u, 0)
                nc.scalar.activation(decay.rearrange("p c t -> p (c t)"), bank[7][:, :], ACT.Exp
                                     ).then_inc(S["decay_exp"], 1)

            def square_y(t):
                passed(act, "y_added", UNITS - 1, max(t - 3, 0))
                if t == 0:
                    passed(act, "wo_lo_done", UNITS - 1, 2)
                else:
                    act.wait_ge(fin_squared, t)
                nc.scalar.activation(w_raw[:, 1, :], y[:, t, :], ACT.Square, accum_out=fss[:, t:t + 1]
                                     ).then_inc(fin_squared, 1)

            def phase_a(u, g):
                for c in range(NCH):
                    passed(act, "qs_done", g, c + 1)
                    passed(act, "o_done", g, c)
                    nc.scalar.activation(qss, bank[3][:, 0:DV], ACT.Identity, scale=e_gc[:, g, c:c + 1]
                                         ).then_inc(S["qs_scaled"], 1)
                    if u is not None and c == 0:
                        evacuate(u, 0)
                    passed(act, "x_done", g, c + 1)
                    passed(act, "av_done", g, c)
                    nc.scalar.activation(xs, bank[4][:, 0:DV], ACT.Copy).then_inc(S["x_out"], 1)
                    if u is not None and c == 2:
                        square_k(u)
                    if c > 0:
                        og_high(g, c - 1)
                    if u is not None:
                        if c == 0:
                            split_hi(u, 2)
                        elif c == 1:
                            tanh(u, 0)
                    passed(act, "o_done", g, c + 1)
                    passed(act, "o_mean", g, c)
                    passed(act, "o_squared", g, c)
                    nc.scalar.activation(junk, o_raw, ACT.Square, accum_out=oss[:, 0:1]
                                         ).then_inc(S["o_squared"], 1)
                    if u is not None:
                        if c == 0:
                            decay_exp(u)
                        elif c == 1:
                            evacuate(u, 1)
                            split_hi(u, 3)
                    if u is None:
                        square_y(c)
                if u is not None:
                    tanh(u, 1)
                    evacuate(u, 2)
                og_high(g, NCH - 1)
                if u is not None:
                    split_hi(u, 4)

            def phase_b(u, last=False):
                passed(act, "q_turned", u, 1)
                passed(act, "q_norm", u, 0)
                for c in range(NCH):
                    if c == 0:
                        passed(act, "k_squared", u, 4)
                    passed(act, "q_squared", u, c)
                    nc.scalar.activation(junk_b, bank[4][:, c * P:(c + 1) * P], ACT.Square,
                                         accum_out=st[:, NCH + c:NCH + c + 1]).then_inc(S["q_squared"], 1)
                evacuate(u, 3)
                split_hi(u, 5)
                split_hi(u, 6)
                tanh(u, 2)
                passed(act, "t_turned", u, 1)
                nc.scalar.activation(u_fin.rearrange("p c t -> p (c t)"), bank[4][:, :], ACT.Copy
                                     ).then_inc(S["u_out"], 1)
                if not last:
                    split_hi(u + 1, 0)
                split_hi(u, 7)
                tanh(u, 3)
                evacuate(u, 4)
                evacuate(u, 5)
                if not last:
                    split_hi(u + 1, 1)
                passed(act, "attn_turned", u, 1)
                nc.scalar.activation(attn_t.rearrange("p c t -> p (c t)"), bank[7][:, :], ACT.Copy
                                     ).then_inc(S["attn_out"], 1)
                passed(act, "v_turned", u, 1)
                passed(act, "scalars_done", u, 1)
                for c in range(NCH):
                    nc.scalar.activation(vt[:, c, :], bank[2 + c // 2][:, (c % 2) * DV:(c % 2 + 1) * DV], ACT.Identity,
                                         scale=sc[:, 2, c:c + 1]).then_inc(S["v_scaled"], 1)

            act.wait_ge(c_in, 16)
            nc.scalar.activation(c_th[:, :], c_col[:, :], ACT.Tanh, scale=0.5).then_inc(c_step, 1)

            def square_x(half):
                act.wait_ge(x_in[half], 16)
                for t in range(4 * half, 4 * half + 4):
                    if t > 0:
                        act.wait_ge(x_squared, t)
                    nc.scalar.activation(hf.rearrange("p s t -> p (s t)"), y[:, t, :], ACT.Square,
                                         accum_out=xss[:, t:t + 1]).then_inc(x_squared, 1)

            def evacuate_h(half, first, last):
                for k in range(first, last):
                    n = 8 * half + k
                    act.wait_ge(x_turned, n + 1)
                    if n >= 2:
                        act.wait_ge(h_split, n - 1)
                    nc.scalar.activation(hf[:, k % 2, :], bank[2 + k % 4][:, :], ACT.Identity,
                                         bias=mod[:, k:k + 1], scale=mod[:, 8 + k:9 + k]).then_inc(h_done, 1)

            square_x(0)
            split_hi(0, 0)
            act.wait_ge(mod_done, 2)
            evacuate_h(0, 0, KT)
            split_hi(0, 1)
            act.wait_ge(h_split, KT)
            square_x(1)
            evacuate(0, 0)
            evacuate_h(1, 0, KT)
            split_hi(0, 2)
            tanh(0, 0)
            act.wait_ge(wba_in, 16)
            nc.scalar.activation(wba_hi, wba_raw, ACT.Copy).then_inc(wba_split, 1)
            evacuate(0, 1)
            split_hi(0, 3)
            tanh(0, 1)
            ba = bank[6][:, 0:P].rearrange("p (c h) -> p h c", h=16)
            act.wait_ge(ba_mm, 1)
            nc.scalar.activation(ba_rows[:, 0:HALF], bank[4][0:16, :], ACT.Copy)
            nc.scalar.activation(ba_rows[:, HALF:], bank[5][0:16, :], ACT.Copy).then_inc(ba_out, 1)
            act.wait_ge(ba_turned, 1)
            nc.scalar.activation(beta[:, :, :].rearrange("p (h s) c -> p h (s c)", s=2), ba[:, 0:8, :],
                                 ACT.Exp, scale=-1.0).then_inc(beta_step, 1)
            act.wait_ge(bias_in, 48)
            nc.scalar.activation(small[:, 16:24], small[:, 0:8], ACT.Exp).then_inc(g_exp, 1)
            act.wait_ge(g_step, 2)
            nc.scalar.activation(e_gc[:, :, :], e_kd[:, :, :], ACT.Exp, scale=-1.0).then_inc(g_exp, 1)
            act.wait_ge(g_exp, 2)
            nc.scalar.activation(e_gl[:, :, :], e_gc[:, :, :], ACT.Ln, bias=1.0).then_inc(g_exp, 1)
            evacuate(0, 2)
            split_hi(0, 4)
            act.wait_ge(sums_mm, 1)
            for i, tab in enumerate((e_gc, e_kd, e_gl)):
                act.wait_ge(g_step, 4)
                nc.scalar.activation(tab[:, :, :].rearrange("p u c -> p (u c)"), bank[4][:, i * 64:(i + 1) * 64],
                                     ACT.Exp).then_inc(tables_done, 1)
            decay_exp(0)
            square_k(0)
            with act.Fori(0, UNITS - 1) as u:
                phase_b(u)
                phase_a(u + 1, u)
            phase_b(UNITS - 1, last=True)
            phase_a(None, UNITS - 1)
            for t in range(4, TILES):
                square_y(t)
        @block.vector
        def _(dve):
            prime(dve, "vector")
            stt = nc.vector.scalar_tensor_tensor

            def convolve(u, m, taps=range(TAPS)):
                head = u // 2
                tile = (8 + head, head, 16 + 2 * head, 17 + 2 * head)[m]
                r = m % 2
                for j in taps:
                    tap = cw[:, bass.ds(tile + 32 * j, 1)]
                    if j == 0:
                        passed(dve, "evacuated", u, m + 1)
                        passed(dve, "qk_done" if m < 2 else "v_turned", u, 0)
                        if m == 0:
                            passed(dve, "kq_done", u, 0)
                        i = nc.vector.tensor_scalar(cv[:, m, :], pre[:, r, 0:HALF], tap, None, ALU.mult)
                    else:
                        passed(dve, "conv_step", u, 4 * m + j)
                        i = stt(out=cv[:, m, :], in0=pre[:, r, j:j + HALF], scalar=tap, in1=cv[:, m, :],
                                op0=ALU.mult, op1=ALU.add)
                    i.then_inc(S["conv_step"], 1)
                if taps[-1] == TAPS - 1:
                    nc.vector.tensor_scalar(tails[:, m, 0:3], pre[:, r, HALF:HALF + 3], even[:, bass.ds(u, 1)],
                                            None, ALU.mult)
                    passed(dve, "conv_step", u, 4 * m + 4)
                    nc.vector.tensor_copy(pre[:, r, 0:3], tails[:, (m + 2) % 4, 0:3]).then_inc(S["conv_done"], 1)

            def silu(u, m):
                passed(dve, "tanh_done", u, m + 1)
                if m < CONVED:
                    t = cv[:, m, :]
                else:
                    passed(dve, "evacuated", u, m + 1)
                    t = zt[:, m - 4, :]
                stt(out=t, in0=th[:, m % 2, :], scalar=1.0, in1=t, op0=ALU.add, op1=ALU.mult
                    ).then_inc(S["silu_done"], 1)

            def norm_o(g, c):
                passed(dve, "o_pow", g, c + 1)
                passed(dve, "o_turned", g, c)
                nc.vector.tensor_scalar(o_n, o_raw, oss[:, 2:3], sc[:, 4, c:c + 1], ALU.mult, ALU.mult
                                        ).then_inc(S["o_scaled"], 1)

            def gate_o(g, c):
                passed(dve, "o_turned", g, c + 1)
                passed(dve, "og_lo_done", g, c)
                if c == 0:
                    passed(dve, "silu_done", g, 6)
                for m in range(2):
                    i = stt(out=og[:, m, :], in0=bank[3][:, m * P:(m + 1) * P], scalar=small[:, 32 + m:33 + m],
                            in1=zt[:, m, c * P:(c + 1) * P], op0=ALU.mult, op1=ALU.mult)
                i.then_inc(S["og_done"], 1)

            def add_y(g, c):
                passed(dve, "out_done", g, c + 1)
                for n in range(2):
                    yt = y_v[:, g % 2, c, n * 512:(n + 1) * 512]
                    i = nc.vector.tensor_tensor(yt, bank[6 + n][:, :], yt, ALU.add)
                i.then_inc(S["y_added"], 1)

            def k_scalars(u):
                passed(dve, "k_norm", u, 1)
                nc.vector.tensor_tensor(sn[:, 0, :], beta[:, u, :], rs[:, 0:NCH], ALU.mult
                                        ).then_inc(S["k_scalar"], 1)
                passed(dve, "k_scalar", u, 1)
                nc.vector.tensor_tensor(sn[:, 1, :], sn[:, 0, :], rs[:, 0:NCH], ALU.mult
                                        ).then_inc(S["k_scalar"], 1)

            def make_n(u):
                passed(dve, "k_scalar", u, 2)
                passed(dve, "decay_done", u, 1)
                passed(dve, "kk_done", u, 1)
                for c in range(NCH):
                    i = stt(out=nmat[:, c, :], in0=bank[5][:, c * P:(c + 1) * P], scalar=sn[:, 1, c:c + 1],
                            in1=decay[:, c, :], op0=ALU.mult, op1=ALU.mult)
                i.then_inc(S["n_done"], 1)

            def decay_k(u):
                passed(dve, "kv_done", u, 0)
                passed(dve, "k_turned", u, 2)
                for c in range(NCH):
                    i = nc.vector.tensor_scalar(kdec[:, c, :], bank[5][:, c * P:(c + 1) * P], e_kd[:, u, c:c + 1],
                                                None, ALU.mult)
                i.then_inc(S["kdec_done"], 1)

            def invert_blocks(u, first, last):
                if first == 0:
                    dve.wait_ge(blk_in, 16 * (u + 1))
                    nc.vector.tensor_copy(blk_y[:, :, :], blk_id[:, :, :]).then_inc(S["base_step"], 1)
                for j in range(first, last):
                    shape = [NBLK * NCH, BLK - 1 - j, j + 1]
                    tmp, below = blk_tmp[:, j + 1:, 0:j + 1], blk_y[:, j + 1:, 0:j + 1]
                    passed(dve, "base_step", u, 2 * j + 1)
                    nc.vector.tensor_tensor(tmp, blk_n[:, j + 1:, j:j + 1].to_broadcast(shape),
                                            blk_y[:, j:j + 1, 0:j + 1].to_broadcast(shape), ALU.mult
                                            ).then_inc(S["base_step"], 1)
                    passed(dve, "base_step", u, 2 * j + 2)
                    nc.vector.tensor_tensor(below, below, tmp, ALU.subtract).then_inc(S["base_step"], 1)

            def norm_y(t):
                if t == 0:
                    dve.wait_ge(fw_in, 16)
                dve.wait_ge(fin_pow, t + 1)
                stt(out=y[:, t, :], in0=y[:, t, :], scalar=frs[:, t:t + 1], in1=w_raw[:, 0, :],
                    op0=ALU.mult, op1=ALU.mult).then_inc(fin_done, 1)

            def phase_a(u, g):
                passed(dve, "qs_done", g, 0)
                nc.vector.tensor_scalar(state[:, :], state[:, :], odd[:, bass.ds(g, 1)], None, ALU.mult
                                        ).then_inc(S["state_done"], 1)
                for c in range(NCH):
                    passed(dve, "ks_done", g, c + 1)
                    passed(dve, "v_scaled", g, c + 1)
                    passed(dve, "x_done", g, c)
                    stt(out=r_rhs, in0=bank[2][:, 0:DV], scalar=sc[:, 1, c:c + 1], in1=vt[:, c, :],
                        op0=ALU.mult, op1=ALU.add).then_inc(S["r_done"], 1)
                    if c > 0:
                        norm_o(g, c - 1)
                    if u is not None:
                        if c == 0:
                            convolve(u, 0, range(0, 2))
                        elif c == 2:
                            convolve(u, 1, range(0, 2))
                        elif c == 3:
                            k_scalars(u)
                            make_n(u)
                            convolve(u, 1, range(2, 3))
                    if c > 0:
                        if u is None:
                            norm_y(c - 1)
                        gate_o(g, c - 1)
                    passed(dve, "kv_done", g, c + 1)
                    passed(dve, "qs_done", g, c + 1)
                    stt(out=state[:, :], in0=state[:, :], scalar=e_gl[:, g, c:c + 1], in1=bank[4][:, DV:2 * DV],
                        op0=ALU.mult, op1=ALU.add).then_inc(S["state_done"], 1)
                    passed(dve, "av_done", g, c + 1)
                    passed(dve, "qs_scaled", g, c + 1)
                    passed(dve, "o_scaled", g, c)
                    nc.vector.tensor_tensor(o_raw, bank[2][:, 0:DV], qss, ALU.add).then_inc(S["o_done"], 1)
                    if u is not None:
                        if c == 0:
                            convolve(u, 0, range(2, 4))
                        elif c == 1:
                            silu(u, 0)
                    if c == 2:
                        add_y(g, 0)
                    passed(dve, "o_squared", g, c + 1)
                    nc.vector.tensor_scalar(oss[:, 1:2], oss[:, 0:1], sc[:, 5, c:c + 1], NORM_EPS,
                                            ALU.mult, ALU.add).then_inc(S["o_mean"], 1)
                    if u is not None and c == 3:
                        convolve(u, 1, range(3, 4))
                norm_o(g, 3)
                add_y(g, 1)
                gate_o(g, 3)
                if u is not None:
                    silu(u, 1)
                    invert_blocks(u, 0, 5)
                add_y(g, 2)
                if u is not None:
                    invert_blocks(u, 5, BLK - 1)
                else:
                    for t in (3, 4, 5, 6):
                        norm_y(t)
                add_y(g, 3)
                if u is None:
                    norm_y(7)

            def phase_b(u, last=False):
                convolve(u, 2)
                dve.wait_ge(t_back, 16 * (u + 1))
                passed(dve, "out_done", u, 0)
                nc.vector.tensor_tensor(tm.rearrange("p c (b w) -> p c b w", w=BLK),
                                        t_comp.unsqueeze(2).to_broadcast([P, NCH, NBLK, BLK]),
                                        diag_mask[:, :].rearrange("p (b w) -> p b w", w=BLK).unsqueeze(1)
                                        .to_broadcast([P, NCH, NBLK, BLK]), ALU.mult).then_inc(S["t_done"], 1)
                decay_k(u)
                passed(dve, "qk_done", u, 1)
                passed(dve, "av_done", u, 0)
                nc.vector.tensor_tensor(attn, bank[2][:, :].rearrange("p (c t) -> p c t", c=NCH), decay, ALU.mult
                                        ).then_inc(S["attn_done"], 1)
                silu(u, 2)
                for lv in range(3):
                    w = BLK << lv
                    nb = 64 // w
                    passed(dve, "merge_p", u, lv + 1)
                    p_out = (pairs(pm[:, lv, :, :], lv)[:, :, :, 1, :] if lv < 2
                             else pm_last.rearrange("p c (b w) -> p c b w", w=w))
                    mask = pair_mask[:, lv, :].rearrange("p (b q w) -> p b q w", q=2, w=w)[:, :, 1, :]
                    nc.vector.tensor_tensor(p_out, halves(bank[5], lv, (lv % 2) * DV),
                                            mask.unsqueeze(1).to_broadcast([P, NCH, nb, w]), ALU.mult
                                            ).then_inc(S["merge_p_out"], 1)
                    if lv < 2:
                        convolve(u, 3, range(2 * lv, 2 * lv + 1))
                    passed(dve, "merge_d", u, lv + 1)
                    d_bank = bank[(6, 4, 6)[lv]]
                    if lv < 2:
                        t_even = pairs(tm, lv)[:, :, :, 0, :]
                        nc.vector.tensor_tensor(t_even, t_even, halves(d_bank, lv), ALU.subtract)
                    u_odd = pairs(u_fin, lv)[:, :, :, 1, :]
                    nc.vector.tensor_tensor(u_odd, u_odd, halves(d_bank, lv, DV), ALU.subtract
                                            ).then_inc(S["merge_d_out"], 1)
                    if lv < 2:
                        convolve(u, 3, range(2 * lv + 1, 2 * lv + 2))
                passed(dve, "q_norm", u, 1)
                passed(dve, "o_mean", u, 0)
                passed(dve, "o_scaled", u, 0)
                nc.vector.tensor_scalar(sc[:, 4, :], rs[:, NCH:2 * NCH], DK ** -0.5, None, ALU.mult
                                        ).then_inc(S["scalar_step"], 1)
                nc.vector.tensor_scalar(sc[:, 2, :], sn[:, 0, :], 0.5, None, ALU.mult)
                stt(out=sc[:, 1, :], in0=sn[:, 1, :], scalar=-1.0, in1=e_gc[:, u, :], op0=ALU.mult, op1=ALU.mult)
                passed(dve, "scalar_step", u, 1)
                stt(out=sc[:, 5, :], in0=sc[:, 4, :], scalar=1.0 / DV, in1=sc[:, 4, :], op0=ALU.mult, op1=ALU.mult
                    ).then_inc(S["scalars_done"], 1)
                silu(u, 3)
                passed(dve, "qs_done", u, 0)
                nc.vector.tensor_copy(kq, cv[:, 0:2, :]).then_inc(S["kq_done"], 1)
                silu(u, 4)
                silu(u, 5)

            def norm_x(half):
                dve.wait_ge(x_pow, half + 1)
                if half == 1:
                    dve.wait_ge(x_turned, KT)
                for t in range(4):
                    nc.vector.tensor_scalar(xn[:, t, :], y[:, 4 * half + t, :],
                                            xrs[:, 4 * half + t:4 * half + t + 1], None, ALU.mult
                                            ).then_inc(xn_done, 1)

            def sum_ada(k, lo, hi, base):
                dve.wait_ge(ada_in[k % 2], 16 * (base // 2 + k // 2 + 1))
                src = (ada_buf if lo == 0 else gate_buf)[:, k % 2, :]
                if k == 0:
                    i = nc.vector.tensor_scalar(ada_acc[:, lo:hi], src, c_th[:, 0:1], None, ALU.mult)
                else:
                    dve.wait_ge(ada_summed, base + k)
                    i = stt(out=ada_acc[:, lo:hi], in0=src, scalar=c_th[:, k:k + 1], in1=ada_acc[:, lo:hi],
                            op0=ALU.mult, op1=ALU.add)
                i.then_inc(ada_summed, 1)

            def split_h(half, first, last):
                for k in range(first, last):
                    n = 8 * half + k
                    dve.wait_ge(h_done, n + 1)
                    nc.vector.tensor_copy(h_hi_v[:, k, half, :], hf[:, k % 2, :]).then_inc(hi_step, 1)
                    dve.wait_ge(hi_step, n + 1)
                    nc.vector.tensor_tensor(h_lo_v[:, k, half, :], hf[:, k % 2, :],
                                            h_hi_v[:, k, half, :].bitcast(F32), ALU.subtract
                                            ).then_inc(h_split, 1)

            dve.wait_ge(rows_turned, 1)
            nc.vector.tensor_copy(cw[:, :], bank[7][:, 0:P])
            nc.vector.tensor_copy(rows_t[:, :], bank[7][:, P:P + 34]).then_inc(rows_out, 1)
            dve.wait_ge(rows_out, 1)
            nc.vector.tensor_scalar(small[:, 32:34], rows_t[:, 32:34], 0.5, None, ALU.mult).then_inc(rows_out, 1)
            dve.wait_ge(c_step, 1)
            stt(out=c_th[:, :], in0=c_th[:, :], scalar=1.0, in1=c_col[:, :], op0=ALU.add, op1=ALU.mult
                ).then_inc(c_step, 1)
            dve.wait_ge(c_step, 2)
            nc.vector.tensor_scalar(c_th[:, :], c_th[:, :], 0.5, None, ALU.mult).then_inc(c_step, 1)
            dve.wait_ge(c_step, 3)
            norm_x(0)
            for k in range(KT):
                sum_ada(k, 0, 2 * D_MODEL, 0)
            dve.wait_ge(mod_mm, 1)
            nc.vector.tensor_tensor(mod[:, 0:16], bank[6][:, 0:16], rows_t[:, 0:16], ALU.add).then_inc(mod_done, 1)
            dve.wait_ge(mod_done, 1)
            stt(out=mod[:, 8:16], in0=mod[:, 8:16], scalar=1.0, in1=rows_t[:, 24:32], op0=ALU.add, op1=ALU.mult
                ).then_inc(mod_done, 1)
            split_h(0, 0, KT)
            norm_x(1)
            convolve(0, 0)
            split_h(1, 0, KT)
            silu(0, 0)
            dve.wait_ge(wba_split, 1)
            nc.vector.tensor_tensor(wba_lo, wba_raw, wba_hi.bitcast(F32), ALU.subtract
                                    ).then_inc(wba_split, 1)
            convolve(0, 1)
            silu(0, 1)
            for k in range(4):
                sum_ada(k, 2 * D_MODEL, 3 * D_MODEL, KT)
            dve.wait_ge(beta_step, 1)
            nc.vector.tensor_scalar(beta[:, :, :], beta[:, :, :], 1.0, None, ALU.add).then_inc(beta_step, 1)
            dve.wait_ge(beta_step, 2)
            nc.vector.reciprocal(beta[:, :, :], beta[:, :, :]).then_inc(beta_step, 1)
            dve.wait_ge(bias_in, 48)
            heads = "p (h s) c -> p h (s c)"
            g_v = g_tab[:, :, :].rearrange(heads, s=2)
            nc.vector.tensor_tensor(g_v, bank[6][:, 0:P].rearrange("p (c h) -> p h c", h=16)[:, 8:16, :],
                                    small[:, 8:16].unsqueeze(2).to_broadcast([P, HEADS, TILES]), ALU.add
                                    ).then_inc(g_step, 1)
            dve.wait_ge(g_step, 1)
            stt(out=e_kd[:, :, :], in0=g_tab[:, :, :], scalar=-1.0, in1=g_tab[:, :, :], op0=ALU.mult, op1=ALU.max
                ).then_inc(g_step, 1)
            dve.wait_ge(g_exp, 3)
            stt(out=g_tab[:, :, :], in0=g_tab[:, :, :], scalar=0.0, in1=e_gl[:, :, :], op0=ALU.max, op1=ALU.add
                ).then_inc(g_step, 1)
            dve.wait_ge(g_step, 3)
            stt(out=g_v, in0=g_v, scalar=-1.0, in1=small[:, 16:24].unsqueeze(2).to_broadcast([P, HEADS, TILES]),
                op0=ALU.mult, op1=ALU.mult).then_inc(g_step, 1)
            k_scalars(0)
            make_n(0)
            for k in range(4, KT):
                sum_ada(k, 2 * D_MODEL, 3 * D_MODEL, KT)
            dve.wait_ge(gate_mm, 1)
            for n in range(2):
                gb = gate_bc[:, n * 512:(n + 1) * 512]
                nc.vector.tensor_tensor(gb, bank[2 + n][:, :], gb, ALU.add).then_inc(gate_done, 1)
            invert_blocks(0, 0, BLK - 1)
            with dve.Fori(0, UNITS - 1) as u:
                phase_b(u)
                phase_a(u + 1, u)
            phase_b(UNITS - 1, last=True)
            phase_a(None, UNITS - 1)
        @block.gpsimd
        def _(pool):
            prime(pool, "gpsimd")
            step = [0]

            def then(i):
                step[0] += 1
                i.then_inc(const_step, 1)
                pool.wait_ge(const_step, step[0])

            def select(ap, pattern, base, channel, op, fill):
                then(nc.gpsimd.affine_select(out=ap, in_=ap, compare_op=op, fill=fill, base=base, pattern=pattern,
                                             channel_multiplier=channel))

            for ap, v in ((ones[:, :], 1.0), (ident[:, :], 0.0), (upto[:, :], 1.0), (after[:, :], 1.0),
                          (lower[:, :], 1.0), (pair_mask[:, :, :], 0.0), (neg_half[:, :], -0.5), (l2_eps4[:, :], 4 * L2_EPS),
                          (even[:, :], 0.0), (odd[:, :], 0.0)):
                nc.gpsimd.memset(ap, v)
            then(nc.gpsimd.memset(blk_id[:, :, :], 0.0))
            select(ident[:, :], [[-1, P]], 0, 1, ALU.not_equal, 1.0)
            nc.gpsimd.sem_inc(consts, 1)
            select(upto[:, :], [[1, P]], 0, -1, ALU.is_ge, 0.0)
            select(after[:, :], [[-1, P]], -1, 1, ALU.is_ge, 0.0)
            select(lower[:, :], [[-1, P]], 0, 1, ALU.is_ge, 0.0)
            select(blk_id[:, :, :], [[1, BLK], [-1, BLK]], 0, 0, ALU.not_equal, 1.0)
            for lv in range(3):
                s = BLK << lv
                n = P // (2 * s)
                m = pair_mask[:, lv, :].rearrange("p (b q w) -> p b q w", q=2, w=s)[:, :, 1, :]
                then(nc.gpsimd.memset(m, 1.0))
                select(m, [[-2 * s, n], [0, s]], 0, 1, ALU.is_ge, 0.0)
                select(m, [[2 * s, n], [0, s]], s - 1, -1, ALU.is_ge, 0.0)
            then(nc.gpsimd.memset(diag_mask[:, :], 1.0))
            d_blocks = diag_mask[:, :].rearrange("p (b w) -> p b w", w=BLK)
            select(d_blocks, [[-BLK, NBLK], [0, BLK]], 0, 1, ALU.is_ge, 0.0)
            select(d_blocks, [[BLK, NBLK], [0, BLK]], BLK - 1, -1, ALU.is_ge, 0.0)
            nc.gpsimd.memset(even[:, 0:UNITS:2], 1.0)
            nc.gpsimd.memset(odd[:, 1:UNITS:2], 1.0)
            nc.gpsimd.memset(pm[:, :, :, :], 0.0)
            nc.gpsimd.memset(state[:, :], 0.0)
            nc.gpsimd.memset(tails[:, :, :], 0.0)
            then(nc.gpsimd.memset(pre[:, :, 0:4], 0.0))
            nc.gpsimd.sem_inc(consts, 1)

            def row_power(half):
                xs_ = xss[:, 4 * half:4 * half + 4]
                pool.wait_ge(x_squared, 4 * half + 4)
                nc.gpsimd.tensor_scalar(xs_, xs_, 1.0 / D_MODEL, NORM_EPS, ALU.mult, ALU.add).then_inc(x_mean, 1)
                pool.wait_ge(x_mean, half + 1)
                nc.gpsimd.tensor_tensor(xrs[:, 4 * half:4 * half + 4], xs_, neg_half[:, 0:4], ALU.pow
                                        ).then_inc(x_pow, 1)

            def split_lo(u, k):
                if k < PIECES:
                    passed(pool, "w_hi_done", u, k + 1)
                    nc.gpsimd.tensor_tensor(w_lo[:, k % 2, :, :], w_raw_k[:, k % 2, :, :],
                                            w_hi[:, k % 2, :, :].bitcast(F32), ALU.subtract
                                            ).then_inc(S["w_lo_done"], 1)
                else:
                    passed(pool, "wo_hi_done", u, k - 5)
                    nc.gpsimd.tensor_tensor(wo_lo[:, k - PIECES, :], w_raw[:, k % 2, :],
                                            wo_hi[:, k - PIECES, :].bitcast(F32), ALU.subtract
                                            ).then_inc(S["wo_lo_done"], 1)

            def gate_tile(u, k):
                tile_landed(pool, u, k)
                nc.gpsimd.tensor_tensor(w_raw[:, k % 2, :], w_raw[:, k % 2, :], gate_bc[:, :], ALU.mult
                                        ).then_inc(S["wo_gated"], 1)

            def mask_g(u):
                pool.wait_ge(t_back, 16 * u)
                nc.gpsimd.tensor_tensor(g_after, after[:, :].unsqueeze(1).to_broadcast([P, NCH, P]),
                                        g_tab[:, u, :].unsqueeze(2).to_broadcast([P, NCH, P]), ALU.mult
                                        ).then_inc(S["g_after_done"], 1)

            def mask_decay(u):
                passed(pool, "decay_exp", u, 1)
                nc.gpsimd.tensor_tensor(decay, decay, lower[:, :].unsqueeze(1).to_broadcast([P, NCH, P]), ALU.mult
                                        ).then_inc(S["decay_done"], 1)

            def norm(u, which, cols):
                passed(pool, f"{which}_squared", u, 4)
                nc.gpsimd.tensor_tensor(rs[:, cols], st[:, cols], l2_eps4[:, 0:NCH], ALU.add
                                        ).then_inc(S[f"{which}_norm_step"], 1)
                passed(pool, f"{which}_norm_step", u, 1)
                nc.gpsimd.tensor_tensor(rs[:, cols], rs[:, cols], neg_half[:, 0:NCH], ALU.pow
                                        ).then_inc(S[f"{which}_norm"], 1)

            def og_low(g, c):
                passed(pool, "og_hi_done", g, c + 1)
                nc.gpsimd.tensor_tensor(og_lo[:, :, :], og, og_hi[:, :, :].bitcast(F32), ALU.subtract
                                        ).then_inc(S["og_lo_done"], 1)

            def row_power_y(t):
                pool.wait_ge(fin_squared, t + 1)
                nc.gpsimd.tensor_scalar(fss[:, t:t + 1], fss[:, t:t + 1], 1.0 / D_MODEL, NORM_EPS, ALU.mult, ALU.add
                                        ).then_inc(fin_step, 1)
                pool.wait_ge(fin_step, t + 1)
                nc.gpsimd.tensor_tensor(frs[:, t:t + 1], fss[:, t:t + 1], neg_half[:, 0:1], ALU.pow
                                        ).then_inc(fin_pow, 1)

            def phase_a(u, g):
                for c in range(NCH):
                    if u is not None:
                        if c == 0:
                            split_lo(u, 2)
                    if c > 0:
                        og_low(g, c - 1)
                    if u is not None and c == 2:
                        passed(pool, "scalars_done", u, 0)
                        norm(u, "k", slice(0, NCH))
                    passed(pool, "o_mean", g, c + 1)
                    nc.gpsimd.tensor_tensor(oss[:, 2:3], oss[:, 1:2], neg_half[:, 0:1], ALU.pow
                                            ).then_inc(S["o_pow"], 1)
                    if u is not None and c == 1:
                        mask_decay(u)
                        split_lo(u, 3)
                    if u is None:
                        row_power_y(c)
                og_low(g, 3)
                if u is not None:
                    split_lo(u, 4)

            def phase_b(u, last=False):
                gate_tile(u, 6)
                split_lo(u, 5)
                split_lo(u, 6)
                norm(u, "q", slice(NCH, 2 * NCH))
                gate_tile(u, 7)
                if not last:
                    split_lo(u + 1, 0)
                split_lo(u, 7)
                if not last:
                    split_lo(u + 1, 1)
                    mask_g(u + 1)

            row_power(0)
            split_lo(0, 0)
            split_lo(0, 1)
            row_power(1)
            split_lo(0, 2)
            split_lo(0, 3)
            pool.wait_ge(g_step, 4)
            mask_g(0)
            mask_decay(0)
            norm(0, "k", slice(0, NCH))
            split_lo(0, 4)
            pool.wait_ge(gate_done, 2)
            with pool.Fori(0, UNITS - 1) as u:
                phase_b(u)
                phase_a(u + 1, u)
            phase_b(UNITS - 1, last=True)
            phase_a(None, UNITS - 1)
            for t in range(4, TILES):
                row_power_y(t)

_INS = ["x", "c", "ada_w", "ada_b", "norm_w", "gdn_w_in", "gdn_conv_w", "gdn_a_log", "gdn_dt_bias",
        "gdn_norm_w", "gdn_w_out", "final_norm_w"]


def kernel(**inputs):
    import numpy as np
    import concourse.bacc as bacc
    from concourse.bass_utils import run_bass_kernel_spmd

    nc = bacc.Bacc("TRN2", target_bir_lowering=False, num_devices=1)
    arrays, args = {}, []
    for name in _INS:
        a = np.ascontiguousarray(inputs[name])
        arrays[f"in_{name}"] = a
        args.append(nc.dram_tensor(f"in_{name}", a.shape, mybir.dt.from_np(a.dtype), kind="ExternalInput").ap())
    args.append(nc.dram_tensor("out_0", (1, SEQ, D_MODEL), F32, kind="ExternalOutput").ap())
    build(nc, *args)
    r = run_bass_kernel_spmd(nc, [arrays], core_ids=[0])
    return r.results[0]["out_0"]
```
